# Optimizing a Trainium2 kernel written in Bass

```python
import math
import jax, jax.numpy as jnp
from jax import lax
import numpy as np

D_MODEL = 1024
BATCH = 1
SEQ = 1024
DEPTH = 1

D_MIX = D_MODEL
D_SSM = D_MIX // 2
SSM_GROUP = 16
N_SSM_GROUPS = D_SSM // SSM_GROUP
SSM_STATE = 64
D_ATTN = D_MIX - D_SSM
N_HEADS = 8
QK_NOPE_DIM = 64
QK_ROPE_DIM = 32
QK_HEAD_DIM = QK_NOPE_DIM + QK_ROPE_DIM
V_HEAD_DIM = D_ATTN // N_HEADS
Q_LORA_RANK = 256
KV_LORA_RANK = 128
ROPE_THETA = 10000.0
Q_BLOCK = 128
D_IN_PROJ = D_SSM + Q_LORA_RANK + KV_LORA_RANK + QK_ROPE_DIM
PEER_HEADS = 8
PEER_N_KEYS = 128
PEER_N_EXPERTS = PEER_N_KEYS * PEER_N_KEYS
PEER_TOPK = 16
PEER_QUERY_DIM = 256
PEER_HALF = PEER_QUERY_DIM // 2
TOKEN_CHUNK = 128
N_ADA = 6
EPS = 1e-6

kernel_name = 'hybrid_s5_mla_peer_block'

def rms_norm(x, gain):
    xf = x.astype(jnp.float32)
    y = xf * lax.rsqrt(jnp.mean(xf * xf, axis=-1, keepdims=True) + EPS)
    return (y * gain.astype(jnp.float32)).astype(x.dtype)

def apply_rope(x, positions):
    half = QK_ROPE_DIM // 2
    inv_freq = ROPE_THETA ** (-jnp.arange(half, dtype=jnp.float32) / half)
    ang = positions.astype(jnp.float32)[:, :, None, None] * inv_freq
    cos, sin = jnp.cos(ang), jnp.sin(ang)
    xf = x.astype(jnp.float32)
    x1, x2 = xf[..., :half], xf[..., half:]
    return jnp.concatenate([x1 * cos - x2 * sin, x2 * cos + x1 * sin], axis=-1).astype(x.dtype)

def _complex_scan_combine(e1, e2):
    a1r, a1i, b1r, b1i = e1
    a2r, a2i, b2r, b2i = e2
    ar = a2r * a1r - a2i * a1i
    ai = a2r * a1i + a2i * a1r
    br = a2r * b1r - a2i * b1i + b2r
    bi = a2r * b1i + a2i * b1r + b2i
    return (ar, ai, br, bi)

def s5_group(u, lam_re, lam_im, log_dt, b_re, b_im, c_re, c_im, d_skip, w_glu, b_glu):
    dtype = u.dtype
    bsz, seq, _ = u.shape
    uf = u.astype(jnp.float32).reshape(bsz, seq, N_SSM_GROUPS, SSM_GROUP)
    lr = lam_re.astype(jnp.float32)
    li = lam_im.astype(jnp.float32)
    dt = jnp.exp(log_dt.astype(jnp.float32))[:, None]
    mag = jnp.exp(lr * dt)
    ar = mag * jnp.cos(li * dt)
    ai = mag * jnp.sin(li * dt)
    den = lr * lr + li * li
    nr, ni = ar - 1.0, ai
    coef_r = ((nr * lr + ni * li) / den)[..., None]
    coef_i = ((ni * lr - nr * li) / den)[..., None]
    br_, bi_ = b_re.astype(jnp.float32), b_im.astype(jnp.float32)
    bbar_r = coef_r * br_ - coef_i * bi_
    bbar_i = coef_r * bi_ + coef_i * br_
    bu_r = jnp.einsum('gpc,bsgc->bsgp', bbar_r, uf)
    bu_i = jnp.einsum('gpc,bsgc->bsgp', bbar_i, uf)
    a_r = jnp.broadcast_to(ar[None, None], (1, seq, N_SSM_GROUPS, SSM_STATE))
    a_i = jnp.broadcast_to(ai[None, None], (1, seq, N_SSM_GROUPS, SSM_STATE))
    _, _, xr, xi = lax.associative_scan(_complex_scan_combine, (a_r, a_i, bu_r, bu_i), axis=1)
    y = (jnp.einsum('gcp,bsgp->bsgc', c_re.astype(jnp.float32), xr)
         - jnp.einsum('gcp,bsgp->bsgc', c_im.astype(jnp.float32), xi)
         + d_skip.astype(jnp.float32) * uf)
    y = jax.nn.gelu(y.reshape(bsz, seq, D_SSM))
    y = y * jax.nn.sigmoid(y @ w_glu.astype(jnp.float32) + b_glu.astype(jnp.float32))
    return y.astype(dtype)

def mla_group(c_q, c_kv, k_rope_raw, positions, q_a_norm, w_uq, kv_a_norm, w_ukv, q_norm, k_norm):
    bsz, seq, _ = c_q.shape
    q = (rms_norm(c_q, q_a_norm) @ w_uq).reshape(bsz, seq, N_HEADS, QK_HEAD_DIM)
    kv = (rms_norm(c_kv, kv_a_norm) @ w_ukv).reshape(bsz, seq, N_HEADS, QK_NOPE_DIM + V_HEAD_DIM)
    k_nope, v = kv[..., :QK_NOPE_DIM], kv[..., QK_NOPE_DIM:]
    k_rope = jnp.broadcast_to(k_rope_raw[:, :, None, :], (bsz, seq, N_HEADS, QK_ROPE_DIM))
    k = jnp.concatenate([k_nope, k_rope], axis=-1)
    q = rms_norm(q, q_norm)
    k = rms_norm(k, k_norm)
    q = jnp.concatenate([q[..., :QK_NOPE_DIM], apply_rope(q[..., QK_NOPE_DIM:], positions)], axis=-1)
    k = jnp.concatenate([k[..., :QK_NOPE_DIM], apply_rope(k[..., QK_NOPE_DIM:], positions)], axis=-1)
    q = q.transpose(0, 2, 1, 3)
    k = k.transpose(0, 2, 1, 3)
    v = v.transpose(0, 2, 1, 3)
    scale = QK_HEAD_DIM ** -0.5
    kpos = jnp.arange(seq)

    def attend_block(i):
        start = i * Q_BLOCK
        qb = lax.dynamic_slice_in_dim(q, start, Q_BLOCK, axis=2)
        s = jnp.einsum('bhqd,bhkd->bhqk', qb, k, preferred_element_type=jnp.float32) * scale
        qpos = start + jnp.arange(Q_BLOCK)
        s = jnp.where(kpos[None, :] <= qpos[:, None], s, -jnp.inf)
        p = jax.nn.softmax(s, axis=-1).astype(v.dtype)
        return jnp.einsum('bhqk,bhkd->bhqd', p, v)

    out = lax.map(attend_block, jnp.arange(seq // Q_BLOCK))
    return out.transpose(1, 0, 3, 2, 4).reshape(bsz, seq, N_HEADS * V_HEAD_DIM)

def peer_ffn(h, w_query, sub_keys, expert_down, expert_up):
    bsz, seq, d = h.shape
    chunks = h.reshape((bsz * seq) // TOKEN_CHUNK, TOKEN_CHUNK, d)

    def chunk_fn(hc):
        q = (hc @ w_query).reshape(TOKEN_CHUNK, PEER_HEADS, 2, PEER_HALF)
        s = jnp.einsum('thpd,pkd->thpk', q, sub_keys, preferred_element_type=jnp.float32)
        s1, i1 = lax.top_k(s[:, :, 0], PEER_TOPK)
        s2, i2 = lax.top_k(s[:, :, 1], PEER_TOPK)
        cand = (s1[..., :, None] + s2[..., None, :]).reshape(TOKEN_CHUNK, PEER_HEADS, PEER_TOPK * PEER_TOPK)
        top_s, top_c = lax.top_k(cand, PEER_TOPK)
        e1 = jnp.take_along_axis(i1, top_c // PEER_TOPK, axis=-1)
        e2 = jnp.take_along_axis(i2, top_c % PEER_TOPK, axis=-1)
        idx = e1 * PEER_N_KEYS + e2
        g = jax.nn.softmax(top_s, axis=-1).astype(hc.dtype)
        u = expert_down[idx]
        a = jax.nn.gelu(jnp.einsum('thkd,td->thk', u, hc))
        return jnp.einsum('thk,thkd->td', g * a, expert_up[idx])

    return lax.map(chunk_fn, chunks).reshape(bsz, seq, d)

def hybrid_layer(x, c, positions, w_ada, b_ada, norm_mix, norm_ffn, w_in,
                 lam_re, lam_im, log_dt, b_re, b_im, c_re, c_im, d_skip, w_glu, b_glu,
                 q_a_norm, w_uq, kv_a_norm, w_ukv, q_norm, k_norm,
                 out_norm_ssm, out_norm_attn, w_out,
                 w_query, sub_keys, expert_down, expert_up):
    mod = (jax.nn.silu(c) @ w_ada + b_ada)[:, None, :]
    shift_m, scale_m, gate_m, shift_f, scale_f, gate_f = jnp.split(mod, N_ADA, axis=-1)
    h = rms_norm(x, norm_mix) * (1.0 + scale_m) + shift_m
    proj = h @ w_in
    u_ssm, c_q, c_kv, k_rope_raw = jnp.split(
        proj, [D_SSM, D_SSM + Q_LORA_RANK, D_SSM + Q_LORA_RANK + KV_LORA_RANK], axis=-1)
    y_ssm = s5_group(u_ssm, lam_re, lam_im, log_dt, b_re, b_im, c_re, c_im, d_skip, w_glu, b_glu)
    y_attn = mla_group(c_q, c_kv, k_rope_raw, positions, q_a_norm, w_uq, kv_a_norm, w_ukv, q_norm, k_norm)
    y = jnp.concatenate([rms_norm(y_ssm, out_norm_ssm), rms_norm(y_attn, out_norm_attn)], axis=-1) @ w_out
    x = x + gate_m * y
    h2 = rms_norm(x, norm_ffn) * (1.0 + scale_f) + shift_f
    return x + gate_f * peer_ffn(h2, w_query, sub_keys, expert_down, expert_up)

def setup_inputs(seed: int = 0) -> dict:
    key = jax.random.key(seed)
    ks = jax.random.split(key, 40)
    L = DEPTH

    def nrm(k, shape, scale):
        return jax.random.normal(k, shape, jnp.float32) * scale

    def gain(k, shape):
        return 1.0 + 0.01 * jax.random.normal(k, shape, jnp.float32)

    G, P, C = N_SSM_GROUPS, SSM_STATE, SSM_GROUP
    n_idx = jnp.arange(P, dtype=jnp.float32)
    lam_im = jnp.broadcast_to(math.pi * n_idx, (L, G, P)) + 0.01 * jax.random.normal(ks[8], (L, G, P), jnp.float32)
    log_dt = jax.random.uniform(ks[9], (L, G), jnp.float32, math.log(1e-3), math.log(1e-1))
    positions = jnp.tile(jnp.arange(SEQ, dtype=jnp.int32)[None, :], (BATCH, 1))
    return {
        'x': nrm(ks[0], (BATCH, SEQ, D_MODEL), 1.0),
        'c': nrm(ks[1], (BATCH, D_MODEL), 1.0),
        'positions': positions,
        'w_ada': nrm(ks[2], (L, D_MODEL, N_ADA * D_MODEL), 0.5 * D_MODEL ** -0.5),
        'b_ada': nrm(ks[3], (L, N_ADA * D_MODEL), 0.01),
        'norm_mix': gain(ks[4], (L, D_MODEL)),
        'norm_ffn': gain(ks[5], (L, D_MODEL)),
        'w_in': nrm(ks[6], (L, D_MODEL, D_IN_PROJ), D_MODEL ** -0.5),
        'lam_re': -0.5 + 0.01 * jax.random.normal(ks[7], (L, G, P), jnp.float32),
        'lam_im': lam_im,
        'log_dt': log_dt,
        'b_re': nrm(ks[10], (L, G, P, C), C ** -0.5),
        'b_im': nrm(ks[11], (L, G, P, C), C ** -0.5),
        'c_re': nrm(ks[12], (L, G, C, P), P ** -0.5),
        'c_im': nrm(ks[13], (L, G, C, P), P ** -0.5),
        'd_skip': nrm(ks[14], (L, G, C), 1.0),
        'w_glu': nrm(ks[15], (L, D_SSM, D_SSM), D_SSM ** -0.5),
        'b_glu': nrm(ks[16], (L, D_SSM), 0.01),
        'q_a_norm': gain(ks[17], (L, Q_LORA_RANK)),
        'w_uq': nrm(ks[18], (L, Q_LORA_RANK, N_HEADS * QK_HEAD_DIM), Q_LORA_RANK ** -0.5),
        'kv_a_norm': gain(ks[19], (L, KV_LORA_RANK)),
        'w_ukv': nrm(ks[20], (L, KV_LORA_RANK, N_HEADS * (QK_NOPE_DIM + V_HEAD_DIM)), KV_LORA_RANK ** -0.5),
        'q_norm': gain(ks[21], (L, QK_HEAD_DIM)),
        'k_norm': gain(ks[22], (L, QK_HEAD_DIM)),
        'out_norm_ssm': gain(ks[23], (L, D_SSM)),
        'out_norm_attn': gain(ks[24], (L, D_ATTN)),
        'w_out': nrm(ks[25], (L, D_MIX, D_MODEL), D_MIX ** -0.5),
        'w_query': nrm(ks[26], (L, D_MODEL, PEER_HEADS * PEER_QUERY_DIM), D_MODEL ** -0.5),
        'sub_keys': nrm(ks[27], (L, 2, PEER_N_KEYS, PEER_HALF), PEER_HALF ** -0.5),
        'expert_down': nrm(ks[28], (L, PEER_N_EXPERTS, D_MODEL), D_MODEL ** -0.5),
        'expert_up': nrm(ks[29], (L, PEER_N_EXPERTS, D_MODEL), 0.5),
    }

def reference(x, c, positions, w_ada, b_ada, norm_mix, norm_ffn, w_in,
              lam_re, lam_im, log_dt, b_re, b_im, c_re, c_im, d_skip, w_glu, b_glu,
              q_a_norm, w_uq, kv_a_norm, w_ukv, q_norm, k_norm,
              out_norm_ssm, out_norm_attn, w_out,
              w_query, sub_keys, expert_down, expert_up):
    for l in range(DEPTH):
        x = hybrid_layer(x, c, positions, w_ada[l], b_ada[l], norm_mix[l], norm_ffn[l], w_in[l],
                         lam_re[l], lam_im[l], log_dt[l], b_re[l], b_im[l], c_re[l], c_im[l],
                         d_skip[l], w_glu[l], b_glu[l],
                         q_a_norm[l], w_uq[l], kv_a_norm[l], w_ukv[l], q_norm[l], k_norm[l],
                         out_norm_ssm[l], out_norm_attn[l], w_out[l],
                         w_query[l], sub_keys[l], expert_down[l], expert_up[l])
    return x


_drawn_inputs = setup_inputs


def setup_inputs(seed=0):
    import zlib

    import numpy as np

    out = dict(_drawn_inputs(seed))
    spreads = {}
    factors = {'b_ada': 3.497,
     'norm_mix': 8.0,
     'norm_ffn': 20.707,
     'lam_re': 64.0,
     'b_glu': 29.241,
     'q_a_norm': 8.0,
     'kv_a_norm': 8.0,
     'q_norm': 8.0,
     'k_norm': 8.0,
     'out_norm_ssm': 38.778,
     'out_norm_attn': 37.497}
    for name, (base, spread) in spreads.items():
        noise = np.random.default_rng([zlib.crc32(name.encode()), seed]).standard_normal(out[name].shape)
        drawn = base * np.exp(spread * noise) if base else spread * noise
        out[name] = __import__('jax').numpy.asarray(drawn.astype(out[name].dtype))
    for name, factor in factors.items():
        out[name] = (out[name] * factor).astype(out[name].dtype)
    return out
```

```python
import math
from contextlib import ExitStack

import numpy as np
import concourse.bass as bass
from concourse import mybir

FP32 = mybir.dt.float32
U32 = mybir.dt.uint32
I32 = mybir.dt.int32
ALU = mybir.AluOpType
ACT = mybir.ActivationFunctionType
AX = mybir.AxisListType

P = 128
D = 1024
KD = D // P
SEQ = 1024
NT = SEQ // P
DS = 512
KS = DS // P
G, NP, C = 32, 64, 16
T2 = G // 2
L = P // C
NC = SEQ // L
H = 8
DN, DR, DV = 64, 32, 64
DQK = DN + DR
HALF = DR // 2
QL, KL = 256, 128
DPROJ = DS + QL + KL + DR
PH, PK, TOPK = 8, 128, 16
EPS = 1e-6
TWO_PI = 2 * math.pi
PI_1 = 6.28125
PI_2 = math.floor((TWO_PI - PI_1) * 2 ** 21) / 2 ** 21
PI_3 = TWO_PI - PI_1 - PI_2
ROUND = 1.5 * 2 ** 23
PI_LOW = 3.1415925

BIG = 24704
KB = 1024

V_C, V_NM, V_NF, V_BA, V_QA, V_KVA, V_OS, V_OA, V_BG, V_END = 0, 8, 16, 24, 72, 74, 75, 79, 83, 87
SHIFT_M, SCALE_M, GATE_M, SHIFT_F, SCALE_F, GATE_F = 0, 8, 16, 24, 32, 40


class Chain:

    def __init__(self, eng, sem, base=0):
        self.eng, self.sem, self.base, self.n = eng, sem, base, 0

    def mark(self, ins):
        self.n += 1
        return ins.then_inc(self.sem, 1)

    def wait(self):
        self.eng.wait_ge(self.sem, self.base + self.n)

    def step(self, ins):
        self.mark(ins)
        self.wait()


class Store:

    def __init__(self, nc):
        self.own = {n: Chain(None, nc.alloc_semaphore(name=f"own_{n}")) for n in ("act", "dve", "pool")}

    def chain(self, eng, name):
        self.own[name].eng = eng
        return self.own[name]


def place(nc, name, shape, kb, dt=FP32):
    return nc.alloc_sbuf_tensor_at(name, shape, dt, offset=BIG + int(kb * KB))


def banks(ctx, nc, name, n):
    return [ctx.enter_context(nc.psum_tensor(f"{name}{i}", [P, 512], FP32)) for i in range(n)]


def bcast(ap, axis, shape):
    return ap.unsqueeze(axis).to_broadcast(shape)


def cmul(nc, ch, outr, outi, ar, ai, br, bi, t):
    v = nc.vector
    ch.mark(v.tensor_tensor(t[0], ar, br, ALU.mult))
    ch.mark(v.tensor_tensor(t[1], ai, bi, ALU.mult))
    ch.mark(v.tensor_tensor(t[2], ar, bi, ALU.mult))
    ch.mark(v.tensor_tensor(t[3], ai, br, ALU.mult))
    ch.wait()
    ch.mark(v.tensor_tensor(outr, t[0], t[1], ALU.subtract))
    ch.mark(v.tensor_tensor(outi, t[2], t[3], ALU.add))
    ch.wait()


def phase_a(nc, A, S):
    ctx = ExitStack()
    S.ident = nc.alloc_sbuf_tensor("ident", [P, P], FP32)
    S.vec = nc.alloc_sbuf_tensor("vec", [P, V_END], FP32)
    S.mod = nc.alloc_sbuf_tensor("mod", [P, 48], FP32)
    S.a_m = nc.alloc_sbuf_tensor("a_m", [P, KD], FP32)
    S.a_f = nc.alloc_sbuf_tensor("a_f", [P, KD], FP32)
    S.rope = nc.alloc_sbuf_tensor("rope", [P, 2, NT, HALF], FP32)
    S.gqk = nc.alloc_sbuf_tensor("gqk", [P, 2, DQK], FP32)
    S.gcol = nc.alloc_sbuf_tensor("gcol", [DQK, 2], FP32)
    S.eps = nc.alloc_sbuf_tensor("eps", [P, 1], FP32)
    S.ssa = nc.alloc_sbuf_tensor("ssa", [P, NT], FP32)
    S.pr_t = place(nc, "pr_t", [P, T2, P], 0)
    S.pi_t = place(nc, "pi_t", [P, T2, P], 8)
    S.toep = place(nc, "toep", [P, G, P], 16)
    S.rr = place(nc, "rr", [P, T2, L + 1, C], 32)
    S.ri = place(nc, "ri", [P, T2, L + 1, C], 41)
    S.wr = place(nc, "wr", [P, T2, NC], 50)
    S.wi = place(nc, "wi", [P, T2, NC], 58)
    S.r8 = place(nc, "r8", [P, T2, NC], 66)
    NR = 3
    wada = place(nc, "wada", [P, NR, KD, 512], 74)
    part = place(nc, "mod_part", [P, 6, 512], 122)
    mrow = place(nc, "mod_row", [1, 2, 512], 190)
    pr = place(nc, "pr", [P, T2, L, C], 135)
    pi = place(nc, "pi", [P, T2, L, C], 143)
    ksb = place(nc, "ksb", [32, T2, P], 151)
    vrow = place(nc, "vrow", [P, P], 159)
    srow = place(nc, "srow", [48, P], 159.5)
    craw = place(nc, "craw", [P, 2, KS, 2, NP], 160)
    ct = place(nc, "ct", [P, 2, T2, C], 164)
    braw = place(nc, "braw", [P, 2, T2, C], 166)
    bbar = place(nc, "bbar", [P, 2, T2, C], 168)
    bbd = place(nc, "bbd", [P, 2, T2, 2, C], 170)
    tmp = place(nc, "tmp", [P, 4, 1024], 174)
    small = lambda *a: ctx.enter_context(nc.sbuf_tensor(*a))
    sm = small("s5small", [P, 24, T2], FP32)
    pw = small("pw", [P, 2, L + 1, T2], FP32)
    wn = small("wn", [P, 2, 2, T2], FP32)
    trig = small("trig", [P, 4, 144], FP32)
    posi = small("posi", [NT, P], I32)
    posf = small("posf", [NT, P], FP32)
    poscol = small("poscol", [P, NT], FP32)
    ldt = small("ldt", [48, 2], FP32)
    freq = small("freq", [P, HALF], FP32)
    halfpi = small("halfpi", [P, 1], FP32)
    one = small("one", [P, 1], FP32)
    silu_c = small("silu_c", [P, KD], FP32)
    scol = small("scol", [P, 48], FP32)
    dcol = small("dcol", [32, T2], FP32)
    eye16 = small("eye16", [32, C], FP32)
    NW = 12

    with ctx:
        pa, pb, pc, pd, pk0, pk1, pk2, pk3 = banks(ctx, nc, "pa", 8)
        sem = lambda n: ctx.enter_context(nc.semaphore(n))
        zeroed, vec_loaded, s_loaded, b_loaded = sem("a_zeroed"), sem("a_vec"), sem("a_s"), sem("a_b")
        gain_loaded, pos_loaded, c_loaded = sem("a_gain"), sem("a_pos"), sem("a_c")
        w_in = [sem(f"a_w{n}") for n in range(NR)]
        w_even_used, w_odd_used, row_out, cols_done = sem("a_weu"), sem("a_wou"), sem("a_rowo"), sem("a_cols")
        w_scaled = sem("a_wsc")
        ident_made, rows_ready, cols_t, c_t = sem("a_ident"), sem("a_rows"), sem("a_colst"), sem("a_ct")
        cols_out, angles_ready, trig_ready, silu_ready = sem("a_colsout"), sem("a_angles"), sem("a_trig"), sem("a_silu")
        dt_ready, mag_ready = sem("a_dt"), sem("a_mag")
        mod_done, p_ready, p_t, p_out = sem("a_mod"), sem("a_pready"), sem("a_pt"), sem("a_pout")
        k_ready, k_done, k_sb, toep_zero, toep_in = sem("a_kready"), sem("a_kdone"), sem("a_ksb"), sem("a_tz"), sem("a_tin")
        block = ctx.enter_context(nc.Block())

        @block.sync
        def _(sp):
            for row, name in ((V_C, "c"), (V_NM, "norm_mix"), (V_NF, "norm_ffn"), (V_BA, "b_ada"), (V_QA, "q_a_norm"),
                              (V_KVA, "kv_a_norm"), (V_OS, "out_norm_ssm"), (V_OA, "out_norm_attn"), (V_BG, "b_glu")):
                src = A[name].rearrange("a (r n) -> (a r) n", n=P)
                sp.dma_start(vrow[row:row + src.shape[0], :], src).then_inc(vec_loaded, 16)
            w = A["w_ada"].rearrange("a (k p) (b n) -> (a b) p k n", p=P, n=512)
            for b in range(NW):
                if b >= NR:
                    sp.wait_ge(w_odd_used if (b - NR) % 2 else w_even_used, (b - NR) // 2 + 1)
                sp.dma_start(wada[:, b % NR], w[b]).then_inc(w_in[b % NR], 16)
            sp.wait_ge(toep_zero, 1)
            sp.wait_ge(k_sb, 1)
            tv = S.toep[:].rearrange("p (t a) n -> p t a n", a=2)
            for j in range(L):
                for a in range(2):
                    sp.dma_start(tv[j * C:(j + 1) * C, :, a, j * C:], ksb[a * C:(a + 1) * C, :, 0:(L - j) * C]).then_inc(toep_in, 16)
            sp.wait_ge(toep_in, 16 * 2 * L)

        @block.gpsimd
        def _(pool):
            own = S.chain(pool, "pool")
            own.step(nc.gpsimd.memset(S.ident[:], 0.0))
            nc.gpsimd.affine_select(out=S.ident[:], in_=S.ident[:], compare_op=ALU.not_equal, fill=1.0, base=0,
                                    pattern=[[-1, P]], channel_multiplier=1).then_inc(ident_made, 1)
            nc.gpsimd.memset(S.eps[:], EPS).then_inc(zeroed, 1)
            nc.gpsimd.memset(halfpi[:], math.pi / 2).then_inc(zeroed, 1)
            nc.gpsimd.memset(bbd[:], 0.0).then_inc(zeroed, 1)
            for f in range(HALF):
                inv = float(np.float32(10000.0) ** np.float32(-np.float32(f) / np.float32(HALF)))
                nc.gpsimd.memset(freq[:, f:f + 1], inv).then_inc(zeroed, 1)
            nc.gpsimd.memset(S.toep[:], 0.0).then_inc(toep_zero, 1)
            nc.gpsimd.memset(one[:], 1.0).then_inc(toep_zero, 1)
            for b in range(1, NW, 2):
                pool.wait_ge(w_scaled, b // 2 + 1)
                wb = wada[:, b % NR]
                own.step(nc.gpsimd.tensor_tensor(wb[:, 0:4], wb[:, 0:4], wb[:, 4:8], ALU.add))
                own.step(nc.gpsimd.tensor_tensor(wb[:, 0:2], wb[:, 0:2], wb[:, 2:4], ALU.add))
                nc.gpsimd.tensor_tensor(part[:, b // 2, :], wb[:, 0], wb[:, 1], ALU.add).then_inc(w_odd_used, 1)

        @block.scalar
        def _(act):
            s = nc.scalar
            act.dma_start(srow[0:16, :], A["lam_re"].rearrange("a (t b) p -> (a t) (b p)", b=2)).then_inc(s_loaded, 16)
            act.dma_start(srow[16:32, :], A["lam_im"].rearrange("a (t b) p -> (a t) (b p)", b=2)).then_inc(s_loaded, 16)
            act.dma_start(ldt[32:48, :], A["log_dt"].rearrange("a (t b) -> (a t) b", b=2)).then_inc(s_loaded, 16)
            act.dma_start(posi[:], A["positions"].rearrange("a (i p) -> (a i) p", p=P)).then_inc(pos_loaded, 16)
            for n, name in enumerate(("c_re", "c_im")):
                src = A[name].rearrange("a (q g) c p -> (a q) (g c) p", g=8)
                for q in range(KS):
                    for dup in range(2):
                        act.dma_start(craw[:, n, q, dup, :], src[q]).then_inc(c_loaded, 16)
            for n, name in enumerate(("b_re", "b_im")):
                act.dma_start(braw[:, n], A[name][0].rearrange("(t b) p c -> b p t c", b=2).rearrange("b p t c -> (b p) t c")).then_inc(b_loaded, 16)
            act.dma_start(dcol[:], A["d_skip"][0].rearrange("(t b) c -> (b c) t", b=2), allow_slow_non_contiguous=True).then_inc(b_loaded, 16)
            for n, name in enumerate(("q_norm", "k_norm")):
                act.dma_start(S.gqk[:, n, :], A[name][0].partition_broadcast(P)).then_inc(gain_loaded, 16)
                act.dma_start(S.gcol[:, n:n + 1], A[name][0].rearrange("(p n) -> p n", n=1), allow_slow_non_contiguous=True).then_inc(gain_loaded, 16)

            def row(b):
                act.wait_ge(w_even_used, b // 2 + 1)
                if b >= 4:
                    act.wait_ge(cols_done, b // 2 - 1)
                s.activation(mrow[:, (b // 2) % 2, :], pa[0:1, :], ACT.Copy).then_inc(row_out, 1)

            def scale(b):
                act.wait_ge(w_in[b % NR], 16 * (b // NR + 1))
                for k in range(KD):
                    last = s.activation(wada[:, b % NR, k], wada[:, b % NR, k], ACT.Copy, scale=silu_c[:, k:k + 1])
                last.then_inc(w_scaled, 1)

            act.wait_ge(cols_out, 1)
            s.activation(silu_c[:], S.vec[:, V_C:V_C + KD], ACT.Silu).then_inc(silu_ready, 1)
            act.wait_ge(silu_ready, 1)
            act.wait_ge(cols_out, 2)
            s.activation(sm[:, 0, :], scol[:, 32:48], ACT.Exp).then_inc(dt_ready, 1)
            scale(1)
            act.wait_ge(angles_ready, 1)
            act.wait_ge(zeroed, 3)
            s.activation(trig[:, 2, :], trig[:, 0, :], ACT.Sin).then_inc(trig_ready, 1)
            s.activation(trig[:, 3, :], trig[:, 1, :], ACT.Sin, bias=halfpi[:], scale=-1.0).then_inc(trig_ready, 1)
            s.activation(sm[:, 3, :], sm[:, 1, :], ACT.Exp).then_inc(mag_ready, 1)
            for b in range(0, NW, 2):
                if b > 0:
                    scale(b + 1)
                row(b)

        @block.tensor
        def _(pe):
            t = nc.tensor
            pe.wait_ge(ident_made, 1)
            pe.wait_ge(vec_loaded, 16 * 9)
            t.transpose(pk0[:, 0:V_END], vrow[0:V_END, :], S.ident[0:V_END, 0:V_END]).then_inc(cols_t, 1)
            pe.wait_ge(rows_ready, 2)
            pe.wait_ge(s_loaded, 48)
            t.transpose(pa[:, 128:176], srow[:], S.ident[0:48, 0:48]).then_inc(cols_t, 1)
            t.transpose(pa[:, 256:256 + NT], posf[:], S.ident[0:NT, 0:NT]).then_inc(cols_t, 1)
            pe.wait_ge(c_loaded, 16 * 16)
            for n, bank in ((0, pb), (1, pc)):
                for q in range(KS):
                    last = t.transpose(bank[:, q * P:(q + 1) * P], craw[:, n, q].rearrange("p a n -> p (a n)"), S.ident[:])
                last.then_inc(c_t, 1)
            pe.wait_ge(silu_ready, 1)

            def row_block(b):
                pe.wait_ge(w_in[b % NR], 16 * (b // NR + 1))
                pe.wait_ge(cols_out, 2)
                if b >= 2:
                    pe.wait_ge(row_out, b // 2)
                for k in range(KD):
                    last = t.matmul(pa[0:1, :], silu_c[:, k:k + 1], wada[:, b % NR, k, :], start=k == 0, stop=k == KD - 1)
                last.then_inc(w_even_used, 1)

            def columns(b):
                pe.wait_ge(toep_zero, 2)
                pe.wait_ge(row_out, b // 2 + 1)
                for n in range(4):
                    t.matmul(pd[:, 4 * b + n:4 * b + n + 1], mrow[:, (b // 2) % 2, n * P:(n + 1) * P], one[0:1, :],
                             start=True, stop=True)
                pe.wait_ge(w_odd_used, b // 2 + 1)
                for n in range(4):
                    last = t.matmul(pd[:, 4 * b + 4 + n:4 * b + 5 + n], part[:, b // 2, n * P:(n + 1) * P], one[:],
                                    start=True, stop=True)
                last.then_inc(cols_done, 1)

            row_block(0)
            for b in range(2, 8, 2):
                row_block(b)
                columns(b - 2)
            pe.wait_ge(k_ready, 1)
            for tt in range(T2):
                o = (pk0, pk1, pk2, pk3)[tt // 4][0:32, (tt % 4) * P:(tt % 4 + 1) * P]
                t.matmul(o, bbd[:, 0, tt].rearrange("p a c -> p (a c)"), S.rr[:, tt, 0:L, :].rearrange("p k c -> p (k c)"),
                         start=True, stop=False)
                last = t.matmul(o, bbd[:, 1, tt].rearrange("p a c -> p (a c)"), S.ri[:, tt, 0:L, :].rearrange("p k c -> p (k c)"),
                                start=False, stop=True)
            last.then_inc(k_done, 1)
            for b in range(8, NW, 2):
                row_block(b)
                columns(b - 2)
            columns(NW - 2)
            pe.wait_ge(p_ready, 1)
            for m, (src, bank) in enumerate(((pr, pb), (pi, pc))):
                for q in range(4):
                    if m * 4 + q >= 2:
                        pe.wait_ge(p_out, m * 4 + q - 1)
                    bank = (pb, pc)[(m * 4 + q) % 2]
                    for i in range(4):
                        last = t.transpose(bank[:, i * P:(i + 1) * P], src[:, 4 * q + i].rearrange("p j c -> p (j c)"), S.ident[:])
                    last.then_inc(p_t, 1)

        @block.vector
        def _(dve):
            v = nc.vector
            ch = S.chain(dve, "dve")
            dve.wait_ge(pos_loaded, 16)
            v.tensor_copy(posf[:], posi[:]).then_inc(rows_ready, 1)
            dve.wait_ge(s_loaded, 48)
            v.tensor_copy(srow[32:48, :].rearrange("p (a n) -> p a n", a=2), bcast(ldt[32:48, :], 2, [16, 2, NP])).then_inc(rows_ready, 1)
            dve.wait_ge(cols_t, 1)
            v.tensor_copy(S.vec[:], pk0[:, 0:V_END]).then_inc(cols_out, 1)
            dve.wait_ge(cols_t, 3)
            ch.step(v.tensor_copy(poscol[:], pa[:, 256:256 + NT]))
            v.tensor_copy(scol[:], pa[:, 128:176]).then_inc(cols_out, 1)
            dve.wait_ge(cols_out, 2)
            dve.wait_ge(zeroed, 3 + HALF)
            DT, LRDT, MAG, T0, T1, T3, T4, DEN, NR, CR, CI, M2, UR, UI = 0, 1, 3, 4, 5, 6, 7, 8, 9, 10, 11, 12, 13, 14
            z = lambda k: sm[:, k, :]
            lr, li = scol[:, 0:16], scol[:, 16:32]
            dve.wait_ge(dt_ready, 1)
            ch.mark(v.tensor_tensor(z(LRDT), lr, z(DT), ALU.mult))
            ch.mark(v.tensor_tensor(trig[:, 0, 128:144], li, z(DT), ALU.mult))
            ch.step(v.tensor_tensor(trig[:, 0, 0:128].rearrange("p (i f) -> p i f", f=HALF), bcast(poscol[:], 2, [P, NT, HALF]),
                                    bcast(freq[:], 1, [P, NT, HALF]), ALU.mult))
            angle, count = trig[:, 0, :], trig[:, 1, :]
            ch.step(v.tensor_scalar(count, angle, 1.0 / TWO_PI, ROUND, ALU.mult, ALU.add))
            ch.step(v.tensor_scalar(count, count, ROUND, None, ALU.subtract))
            for part in (PI_1, PI_2, PI_3):
                ch.step(v.scalar_tensor_tensor(angle, count, -part, angle, ALU.mult, ALU.add))
            ch.step(v.tensor_scalar(angle, angle, PI_LOW, -PI_LOW, ALU.min, ALU.max))
            v.scalar_tensor_tensor(count, angle, -1.0, angle, ALU.mult, ALU.max).then_inc(angles_ready, 1)
            ch.mark(v.tensor_tensor(z(T0), lr, lr, ALU.mult))
            ch.mark(v.tensor_tensor(z(T1), li, li, ALU.mult))
            ch.wait()
            ch.step(v.tensor_tensor(z(DEN), z(T0), z(T1), ALU.add))
            ch.step(v.reciprocal(z(DEN), z(DEN)))
            dve.wait_ge(trig_ready, 2)
            for n in range(2):
                ch.mark(v.tensor_copy(S.rope[:, n].rearrange("p i f -> p (i f)"), trig[:, 2 + n, 0:128]))
            usin, ucos = trig[:, 2, 128:144], trig[:, 3, 128:144]
            pk = lambda c, a, b: pw[:, c, a:b, :]
            ch.mark(v.memset(pw[:, 0, 0, :], 1.0))
            ch.mark(v.memset(pw[:, 1, 0, :], 0.0))
            dve.wait_ge(mag_ready, 1)
            ch.mark(v.tensor_tensor(pw[:, 0, 1, :], z(MAG), ucos, ALU.mult))
            ch.mark(v.tensor_tensor(pw[:, 1, 1, :], z(MAG), usin, ALU.mult))
            ch.wait()
            tv = lambda n: [tmp[:, k, 0:n * T2].rearrange("p (n t) -> p n t", t=T2) for k in range(4)]
            for n in (1, 2, 4):
                cmul(nc, ch, pk(0, n + 1, 2 * n + 1), pk(1, n + 1, 2 * n + 1), pk(0, 1, n + 1), pk(1, 1, n + 1),
                     pk(0, n, n + 1).to_broadcast([P, n, T2]), pk(1, n, n + 1).to_broadcast([P, n, T2]), tv(n))
            ar, ai = pw[:, 0, 1, :], pw[:, 1, 1, :]
            ch.step(v.tensor_scalar(z(NR), ar, 1.0, None, ALU.subtract))
            ch.mark(v.tensor_tensor(z(T0), z(NR), lr, ALU.mult))
            ch.mark(v.tensor_tensor(z(T1), ai, li, ALU.mult))
            ch.mark(v.tensor_tensor(z(T3), ai, lr, ALU.mult))
            ch.mark(v.tensor_tensor(z(T4), z(NR), li, ALU.mult))
            ch.wait()
            ch.mark(v.tensor_tensor(z(CR), z(T0), z(T1), ALU.add))
            ch.mark(v.tensor_tensor(z(CI), z(T3), z(T4), ALU.subtract))
            ch.wait()
            ch.mark(v.tensor_tensor(z(CR), z(CR), z(DEN), ALU.mult))
            ch.mark(v.tensor_tensor(z(CI), z(CI), z(DEN), ALU.mult))
            ch.wait()
            dve.wait_ge(b_loaded, 48)
            tc = [tmp[:, k, 0:256].rearrange("p (t c) -> p t c", c=C) for k in range(4)]
            on_c = lambda ap: bcast(ap, 2, [P, T2, C])
            cmul(nc, ch, bbar[:, 0], bbar[:, 1], braw[:, 0], braw[:, 1], on_c(z(CR)), on_c(z(CI)), tc)
            for n in range(2):
                for a in range(2):
                    ch.mark(v.tensor_copy(bbd[a * NP:(a + 1) * NP, n, :, a, :], bbar[a * NP:(a + 1) * NP, n]))
            dve.wait_ge(c_t, 2)
            for n, bank in ((0, pb), (1, pc)):
                for a in range(2):
                    src = bank[a * NP:(a + 1) * NP, :].rearrange("p (t b c) -> p t b c", b=2, c=C)[:, :, a, :]
                    ch.mark(v.tensor_copy(ct[a * NP:(a + 1) * NP, n], src))
            ch.wait()
            for k in range(L + 1):
                pr_k, pi_k = on_c(pw[:, 0, k, :]), on_c(pw[:, 1, k, :])
                ch.mark(v.tensor_tensor(tc[0], ct[:, 0], pr_k, ALU.mult))
                ch.mark(v.tensor_tensor(tc[1], ct[:, 1], pi_k, ALU.mult))
                ch.mark(v.tensor_tensor(tc[2], ct[:, 0], pi_k, ALU.mult))
                ch.mark(v.tensor_tensor(tc[3], ct[:, 1], pr_k, ALU.mult))
                ch.wait()
                ch.mark(v.tensor_tensor(S.rr[:, :, k, :], tc[0], tc[1], ALU.subtract))
                ch.mark(v.scalar_tensor_tensor(S.ri[:, :, k, :], tc[2], -1.0, tc[3], ALU.mult, ALU.subtract))
                ch.wait()
            v.tensor_tensor(eye16[:], S.ident[0:32, 0:C], S.ident[0:32, C:2 * C], ALU.add).then_inc(k_ready, 1)
            for j in range(L):
                cmul(nc, ch, pr[:, :, j, :], pi[:, :, j, :], bbar[:, 0], bbar[:, 1],
                     on_c(pw[:, 0, L - 1 - j, :]), on_c(pw[:, 1, L - 1 - j, :]), tc)
            v.tensor_copy(z(UR), ucos).then_inc(p_ready, 1)
            ch.step(v.tensor_copy(z(UI), usin))
            dve.wait_ge(k_done, 1)
            for n, bank in enumerate((pk0, pk1, pk2, pk3)):
                ch.mark(v.tensor_copy(ksb[:, 4 * n:4 * n + 4, :], bank[0:32, :].rearrange("p (t n) -> p t n", t=4)))
            dve.wait_ge(k_ready, 1)
            ch.step(v.tensor_tensor(tc[0][0:32], bcast(dcol[:], 2, [32, T2, C]), bcast(eye16[:], 1, [32, T2, C]), ALU.mult))
            v.tensor_tensor(ksb[:, :, 0:C], ksb[:, :, 0:C], tc[0][0:32], ALU.add).then_inc(k_sb, 1)
            dve.wait_ge(p_ready, 1)
            ch.step(v.tensor_tensor(z(M2), z(MAG), z(MAG), ALU.mult))
            ch.step(v.tensor_tensor(z(M2), z(M2), z(M2), ALU.mult))
            ch.step(v.tensor_tensor(z(M2), z(M2), z(M2), ALU.mult))
            ch.step(v.tensor_copy(S.r8[:], bcast(z(M2), 2, [P, T2, NC])))
            ch.mark(v.memset(S.r8[:, :, 0:1], 0.0))
            tt = [tmp[:, k, 0:T2] for k in range(4)]
            cmul(nc, ch, wn[:, 0, 0, :], wn[:, 0, 1, :], z(UR), z(UI), z(UR), z(UI), tt)
            cmul(nc, ch, wn[:, 1, 0, :], wn[:, 1, 1, :], wn[:, 0, 0, :], wn[:, 0, 1, :], wn[:, 0, 0, :], wn[:, 0, 1, :], tt)
            cmul(nc, ch, wn[:, 0, 0, :], wn[:, 0, 1, :], wn[:, 1, 0, :], wn[:, 1, 1, :], wn[:, 1, 0, :], wn[:, 1, 1, :], tt)
            ch.mark(v.memset(S.wr[:, :, 0:1], 1.0))
            ch.mark(v.memset(S.wi[:, :, 0:1], 0.0))
            ch.wait()
            n, at = 1, 0
            while n < NC:
                tn = [tmp[:, k, 0:T2 * n].rearrange("p (t c) -> p t c", c=n) for k in range(4)]
                wnr, wni = wn[:, at, 0, :], wn[:, at, 1, :]
                cmul(nc, ch, S.wr[:, :, n:2 * n], S.wi[:, :, n:2 * n], S.wr[:, :, 0:n], S.wi[:, :, 0:n],
                     bcast(wnr, 2, [P, T2, n]), bcast(wni, 2, [P, T2, n]), tn)
                cmul(nc, ch, wn[:, 1 - at, 0, :], wn[:, 1 - at, 1, :], wnr, wni, wnr, wni, tt)
                n, at = 2 * n, 1 - at
            for m in range(8):
                dve.wait_ge(p_t, m + 1)
                dst = (S.pr_t, S.pi_t)[m // 4]
                v.tensor_copy(dst[:, 4 * (m % 4):4 * (m % 4) + 4, :], (pb, pc)[m % 2][:].rearrange("p (t n) -> p t n", n=P)).then_inc(p_out, 1)
            dve.wait_ge(cols_done, NW // 2)
            dve.wait_ge(cols_out, 2)
            ch.step(v.tensor_tensor(S.mod[:], pd[:, 0:48], S.vec[:, V_BA:V_BA + 48], ALU.add))
            for a, scale, norm in ((S.a_m, SCALE_M, V_NM), (S.a_f, SCALE_F, V_NF)):
                ch.step(v.scalar_tensor_tensor(a[:], S.mod[:, scale:scale + KD], 1.0, S.vec[:, norm:norm + KD], ALU.add, ALU.mult))
            dve.wait_ge(gain_loaded, 64)
            ch.step(v.memset(S.gcol[DN:DQK, :], 1.0))


def phase_b(nc, A, S):
    S.ug = place(nc, "ug", [P, G, NC], 74)
    S.ct = place(nc, "ct_lat", [P, 3, SEQ], 90)
    S.kr = place(nc, "kr", [P, NT, DR], 102)
    ht = place(nc, "ht", [P, KD, SEQ], 103)
    win = place(nc, "win", [P, KD, DPROJ], 135)
    up = place(nc, "up", [P, G, L, C], 165)
    xt = place(nc, "xt", [P, 4, D], 181)
    junk = place(nc, "junk_b", [P, D], 181 - 16)
    clat = place(nc, "clat", [P, 2, 3, P], 169)

    with ExitStack() as ctx:
        st = ctx.enter_context(nc.sbuf_tensor("stat_b", [P, NT, 6], FP32))
        ta, tb, m0, m1, cb, u0, u1 = banks(ctx, nc, "pb", 7)
        sem = lambda n: ctx.enter_context(nc.semaphore(n))
        x_in = [sem(f"b_xin{n}") for n in range(4)]
        w_mla_in, w_ssm_in = sem("b_wmla"), sem("b_wssm")
        std_ready, xs_ready, xt_done, ha_out, hb_out = sem("b_std"), sem("b_xs"), sem("b_xt"), sem("b_ha"), sem("b_hb")
        mla_done, cstd_ready, c_scaled, ct_done, ct_out = sem("b_mla"), sem("b_cstd"), sem("b_csc"), sem("b_ctd"), sem("b_cto")
        u_done, u_out_a, u_out_d = sem("b_u"), sem("b_ua"), sem("b_ud")
        g_done, g_out_a, g_out_d = sem("b_g"), sem("b_ga"), sem("b_gd")
        block = ctx.enter_context(nc.Block())
        tile = lambda i: slice(i * P, (i + 1) * P)

        @block.sync
        def _(sp):
            w = A["w_in"][0].rearrange("(k p) n -> p k n", p=P)
            x = A["x"][0].rearrange("(i p) d -> i p d", p=P)
            for i in range(NT):
                if i >= 4:
                    sp.wait_ge(xt_done, i - 3)
                sp.dma_start(xt[:, i % 4, :], x[i]).then_inc(x_in[i % 4], 16)
                if i == 1:
                    sp.dma_start(win[:, :, DS:], w[:, :, DS:]).then_inc(w_mla_in, 16)
                if i == 3:
                    sp.dma_start(win[:, :, 0:DS], w[:, :, 0:DS]).then_inc(w_ssm_in, 16)

        @block.scalar
        def _(act):
            s = nc.scalar
            own = S.chain(act, "act")
            for it in range(NT + 3):
                i = it
                if i < NT:
                    act.wait_ge(x_in[i % 4], 16 * (i // 4 + 1))
                    own.step(s.activation(junk[:], xt[:, i % 4, :], ACT.Square, accum_out=st[:, i, 0:1]))
                    s.activation(st[:, i, 1:2], st[:, i, 0:1], ACT.Sqrt, scale=1.0 / D, bias=S.eps[:]).then_inc(std_ready, 1)
                i = it - 1
                if 0 <= i < NT:
                    act.wait_ge(xt_done, i + 1)
                    for k in range(4):
                        last = s.activation(ht[:, k, tile(i)], ta[:, k * P:(k + 1) * P], ACT.Identity,
                                            scale=S.a_m[:, k:k + 1], bias=S.mod[:, SHIFT_M + k:SHIFT_M + k + 1])
                    last.then_inc(ha_out, 1)
                i = it - 2
                if 0 <= i < NT:
                    act.wait_ge(mla_done, i + 1)
                    bank = (m0, m1)[i % 2]
                    own.step(s.activation(junk[:, 0:QL], bank[:, 0:QL], ACT.Square, accum_out=st[:, i, 2:3]))
                    own.step(s.activation(junk[:, 0:KL], bank[:, QL:QL + KL], ACT.Square, accum_out=st[:, i, 3:4]))
                    s.activation(st[:, i, 4:5], st[:, i, 2:3], ACT.Sqrt, scale=1.0 / QL, bias=S.eps[:]).then_inc(cstd_ready, 1)
                    s.activation(st[:, i, 5:6], st[:, i, 3:4], ACT.Sqrt, scale=1.0 / KL, bias=S.eps[:]).then_inc(cstd_ready, 1)
                i = it - 3
                if 0 <= i < NT:
                    act.wait_ge(ct_done, i + 1)
                    for n in range(3):
                        last = s.activation(S.ct[:, n, tile(i)], cb[:, n * P:(n + 1) * P], ACT.Copy,
                                            scale=S.vec[:, V_QA + n:V_QA + n + 1])
                    last.then_inc(ct_out, 1)
            for j in range(0, L, 2):
                act.wait_ge(u_done, j + 1)
                s.activation(up[:, :, j, :], u0[:].rearrange("p (g c) -> p g c", c=C), ACT.Copy).then_inc(u_out_a, 1)
            for q in range(0, G // 4, 2):
                act.wait_ge(g_done, q + 1)
                s.activation(S.ug[:, 4 * q:4 * q + 4, :], ta[:].rearrange("p (g n) -> p g n", g=4), ACT.Copy).then_inc(g_out_a, 1)

        @block.vector
        def _(dve):
            v = nc.vector
            own = S.chain(dve, "dve")
            for it in range(NT + 3):
                i = it
                if i < NT:
                    dve.wait_ge(std_ready, i + 1)
                    own.step(v.reciprocal(st[:, i, 1:2], st[:, i, 1:2]))
                    v.tensor_scalar(xt[:, i % 4, :], xt[:, i % 4, :], st[:, i, 1:2], None, ALU.mult).then_inc(xs_ready, 1)
                i = it - 1
                if 0 <= i < NT:
                    dve.wait_ge(xt_done, i + 1)
                    for k in range(4, KD):
                        last = v.tensor_scalar(ht[:, k, tile(i)], tb[:, (k - 4) * P:(k - 3) * P], S.a_m[:, k:k + 1],
                                               S.mod[:, SHIFT_M + k:SHIFT_M + k + 1], ALU.mult, ALU.add)
                    last.then_inc(hb_out, 1)
                i = it - 2
                if 0 <= i < NT:
                    dve.wait_ge(cstd_ready, 2 * i + 2)
                    own.step(v.reciprocal(st[:, i, 4:6], st[:, i, 4:6]))
                    bank = (m0, m1)[i % 2]
                    if i >= 2:
                        dve.wait_ge(ct_done, i - 1)
                    cl = clat[:, i % 2].rearrange("p n m -> p (n m)")
                    v.tensor_scalar(cl[:, 0:QL], bank[:, 0:QL], st[:, i, 4:5], None, ALU.mult).then_inc(c_scaled, 1)
                    v.tensor_scalar(cl[:, QL:QL + KL], bank[:, QL:QL + KL], st[:, i, 5:6], None, ALU.mult).then_inc(c_scaled, 1)
                    v.tensor_copy(S.kr[:, i, :], bank[:, QL + KL:QL + KL + DR]).then_inc(c_scaled, 1)
            for j in range(1, L, 2):
                dve.wait_ge(u_done, j + 1)
                v.tensor_copy(up[:, :, j, :], u1[:].rearrange("p (g c) -> p g c", c=C)).then_inc(u_out_d, 1)
            for q in range(1, G // 4, 2):
                dve.wait_ge(g_done, q + 1)
                v.tensor_copy(S.ug[:, 4 * q:4 * q + 4, :], tb[:].rearrange("p (g n) -> p g n", g=4)).then_inc(g_out_d, 1)

        @block.tensor
        def _(pe):
            t = nc.tensor
            for it in range(NT + 2):
                i = it
                if i < NT:
                    pe.wait_ge(xs_ready, i + 1)
                    if i >= 1:
                        pe.wait_ge(ha_out, i)
                        pe.wait_ge(hb_out, i)
                    for k in range(KD):
                        last = t.transpose((ta, tb)[k // 4][:, (k % 4) * P:(k % 4 + 1) * P],
                                           xt[:, i % 4, k * P:(k + 1) * P], S.ident[:])
                    last.then_inc(xt_done, 1)
                i = it - 1
                if 0 <= i < NT:
                    if i == 0:
                        pe.wait_ge(w_mla_in, 16)
                    pe.wait_ge(ha_out, i + 1)
                    pe.wait_ge(hb_out, i + 1)
                    if i >= 2:
                        pe.wait_ge(c_scaled, 3 * (i - 1))
                    for k in range(KD):
                        last = t.matmul((m0, m1)[i % 2][:, 0:DPROJ - DS], ht[:, k, tile(i)], win[:, k, DS:],
                                        start=k == 0, stop=k == KD - 1)
                    last.then_inc(mla_done, 1)
                i = it - 2
                if 0 <= i < NT:
                    pe.wait_ge(c_scaled, 3 * (i + 1))
                    if i >= 1:
                        pe.wait_ge(ct_out, i)
                    for n in range(3):
                        last = t.transpose(cb[:, n * P:(n + 1) * P], clat[:, i % 2, n, :], S.ident[:])
                    last.then_inc(ct_done, 1)
            pe.wait_ge(w_ssm_in, 16)
            for j in range(L):
                if j >= 2:
                    pe.wait_ge((u_out_a, u_out_d)[j % 2], j // 2)
                for k in range(KD):
                    last = t.matmul((u0, u1)[j % 2][:], ht[:, k, j::L], win[:, k, 0:DS], start=k == 0, stop=k == KD - 1)
                last.then_inc(u_done, 1)
            pe.wait_ge(u_out_a, L // 2)
            pe.wait_ge(u_out_d, L // 2)
            for q in range(G // 4):
                if q >= 2:
                    pe.wait_ge((g_out_a, g_out_d)[q % 2], q // 2)
                for n in range(4):
                    last = t.transpose((ta, tb)[q % 2][:, n * P:(n + 1) * P], up[:, 4 * q + n].rearrange("p j c -> p (j c)"), S.ident[:])
                last.then_inc(g_done, 1)


def phase_c(nc, A, S):
    TQ = 4
    W = TQ * NC
    S.yst = place(nc, "yst", [P, KS, SEQ], 103)
    tv = place(nc, "rot_v", [P, 4, W], 103)
    sp_ = place(nc, "rotated", [P, 2, 2, W], 111)
    z = place(nc, "scanned", [P, 2, 2, W], 119)
    tp = place(nc, "rot_p", [P, 4, W], 127)
    xs = place(nc, "xstate", [P, 2, 2, 2, W], 135)
    yp = place(nc, "yp", [P, L, DS], 151)
    yt = place(nc, "yt", [P, KS, SEQ], 167)
    wglu = place(nc, "wglu", [P, KS, DS], 183)
    gate = place(nc, "gate", [P, 2, 512], 191)

    with ExitStack() as ctx:
        r0, r1, i0, i1, y0, y1, t0, t1 = banks(ctx, nc, "pcc", 8)
        sem = lambda n: ctx.enter_context(nc.semaphore(n))
        w_in, s_done, s_read, z_ready, x_ready, x_zero = sem("c_w"), sem("c_s"), sem("c_sread"), sem("c_z"), sem("c_x"), sem("c_xz")
        y_done, y_out, tr_done, tr_out_a, tr_out_d = sem("c_y"), sem("c_yout"), sem("c_tr"), sem("c_tra"), sem("c_trd")
        t2_done, t2_out_a, t2_out_d = sem("c_t2"), sem("c_t2a"), sem("c_t2d")
        g_done, g_out, g_mul = sem("c_g"), sem("c_gout"), sem("c_gmul")
        block = ctx.enter_context(nc.Block())
        quarter = lambda ap, q: ap[:, q * TQ:(q + 1) * TQ, :].rearrange("p t c -> p (t c)")

        @block.sync
        def _(sp):
            sp.dma_start(wglu[:], A["w_glu"][0].rearrange("(k p) n -> p k n", p=P)).then_inc(w_in, 16)

        @block.tensor
        def _(pe):
            t = nc.tensor

            def states(q):
                if q >= 2:
                    pe.wait_ge(s_read, q - 1)
                for coef, bank in ((S.pr_t, (r0, r1)[q % 2]), (S.pi_t, (i0, i1)[q % 2])):
                    for n in range(TQ):
                        tt = q * TQ + n
                        for a in range(2):
                            last = t.matmul(bank[a * NP:(a + 1) * NP, n * NC:(n + 1) * NC], coef[:, tt, a * NP:(a + 1) * NP],
                                            S.ug[:, 2 * tt + a, :], start=True, stop=True)
                last.then_inc(s_done, 1)

            def outputs(q):
                pe.wait_ge(x_ready, 4 * (q + 1))
                if q >= 1:
                    pe.wait_ge(y_out, 2 * q)
                for half in range(2):
                    for n in range(4):
                        g = 2 * TQ * q + 4 * half + n
                        tt, a, nl = g // 2, g % 2, (g // 2) % TQ
                        o = (y0, y1)[half][:, n * NC:(n + 1) * NC]
                        t.matmul(o, S.toep[:, g, :], S.ug[:, g, :], start=True, stop=False)
                        t.matmul(o, S.rr[:, tt, 1:L + 1, :].rearrange("p k c -> p (k c)"),
                                 xs[:, q % 2, 0, a, nl * NC:(nl + 1) * NC], start=False, stop=False)
                        last = t.matmul(o, S.ri[:, tt, 1:L + 1, :].rearrange("p k c -> p (k c)"),
                                        xs[:, q % 2, 1, a, nl * NC:(nl + 1) * NC], start=False, stop=True)
                    last.then_inc(y_done, 1)

            states(0)
            states(1)
            for q in range(4):
                outputs(q)
                if q < 2:
                    states(q + 2)
            pe.wait_ge(y_out, 8)
            for b in range(8):
                if b >= 2:
                    pe.wait_ge((tr_out_a, tr_out_d)[b % 2], b // 2)
                for n in range(4):
                    last = t.transpose((t0, t1)[b % 2][:, n * P:(n + 1) * P], S.ug[:, 4 * b + n, :], S.ident[:])
                last.then_inc(tr_done, 1)
            pe.wait_ge(tr_out_a, 4)
            pe.wait_ge(tr_out_d, 4)
            for b in range(8):
                if b >= 2:
                    pe.wait_ge((t2_out_a, t2_out_d)[b % 2], b // 2)
                for n in range(4):
                    last = t.transpose((t0, t1)[b % 2][:, n * P:(n + 1) * P],
                                       yp[:, 4 * (b % 2) + n, (b // 2) * P:(b // 2 + 1) * P], S.ident[:])
                last.then_inc(t2_done, 1)
            pe.wait_ge(w_in, 16)
            pe.wait_ge(t2_out_a, 4)
            pe.wait_ge(t2_out_d, 4)
            for b in range(8):
                if b >= 2:
                    pe.wait_ge(g_out, b - 1)
                for k in range(KS):
                    last = t.matmul((y0, y1)[b % 2][:], wglu[:, k, (b // 2) * P:(b // 2 + 1) * P],
                                    yt[:, k, (b % 2) * 512:(b % 2 + 1) * 512], start=k == 0, stop=k == KS - 1)
                last.then_inc(g_done, 1)

        @block.vector
        def _(dve):
            v = nc.vector
            own = S.chain(dve, "dve")
            for q in range(4):
                wr, wi = quarter(S.wr, q), quarter(S.wi, q)
                dve.wait_ge(s_done, q + 1)
                sr, si = (r0, r1)[q % 2][:], (i0, i1)[q % 2][:]
                own.mark(v.tensor_tensor(tv[:, 0], sr, wr, ALU.mult))
                own.mark(v.tensor_tensor(tv[:, 1], si, wi, ALU.mult))
                own.mark(v.tensor_tensor(tv[:, 2], si, wr, ALU.mult))
                own.mark(v.tensor_tensor(tv[:, 3], sr, wi, ALU.mult))
                own.wait()
                own.mark(v.tensor_tensor(sp_[:, q % 2, 0], tv[:, 0], tv[:, 1], ALU.add))
                v.tensor_tensor(sp_[:, q % 2, 1], tv[:, 2], tv[:, 3], ALU.subtract).then_inc(s_read, 1)
                own.wait()
                dve.wait_ge(s_read, q + 1)
                if q >= 2:
                    dve.wait_ge(x_ready, 4 * (q - 1))
                for n in range(2):
                    v.tensor_tensor_scan(z[:, q % 2, n], quarter(S.r8, q), sp_[:, q % 2, n], 0.0, ALU.mult, ALU.add).then_inc(z_ready, 1)
            for b in range(1, 8, 2):
                dve.wait_ge(tr_done, b + 1)
                v.tensor_copy(yp[:, :, 4 * b * C:4 * (b + 1) * C].rearrange("p i (g c) -> p i g c", c=C),
                              t1[:].rearrange("p (g i c) -> p i g c", g=4, c=C)).then_inc(tr_out_d, 1)
            for b in range(1, 8, 2):
                dve.wait_ge(t2_done, b + 1)
                v.tensor_copy(yt[:, b // 2, :].rearrange("p (c i) -> p i c", i=L)[:, 4:8, :],
                              t1[:].rearrange("p (i c) -> p i c", i=4)).then_inc(t2_out_d, 1)
            for b in range(8):
                dve.wait_ge(g_out, b + 1)
                sl = slice((b % 2) * 512, (b % 2 + 1) * 512)
                v.tensor_tensor(S.yst[:, b // 2, sl], yt[:, b // 2, sl], gate[:, b % 2], ALU.mult).then_inc(g_mul, 1)

        @block.gpsimd
        def _(pool):
            p = nc.gpsimd
            own = S.chain(pool, "pool")
            own.step(p.memset(xs[:], 0.0))
            for q in range(4):
                wr, wi = quarter(S.wr, q), quarter(S.wi, q)
                zr, zi = z[:, q % 2, 0], z[:, q % 2, 1]
                pool.wait_ge(z_ready, 2 * q + 2)
                if q >= 1:
                    pool.wait_ge(x_ready, 4 * q)
                own.mark(p.tensor_tensor(tp[:, 0], zr, wr, ALU.mult))
                own.mark(p.tensor_tensor(tp[:, 1], zi, wi, ALU.mult))
                own.mark(p.tensor_tensor(tp[:, 2], zi, wr, ALU.mult))
                own.mark(p.tensor_tensor(tp[:, 3], zr, wi, ALU.mult))
                own.wait()
                if q >= 2:
                    pool.wait_ge(y_done, 2 * (q - 1))
                t3 = lambda k, a: tp[a * NP:(a + 1) * NP, k].rearrange("p (t c) -> p t c", c=NC)[:, :, 0:NC - 1]
                x3 = lambda n, a: xs[a * NP:(a + 1) * NP, q % 2, n, a].rearrange("p (t c) -> p t c", c=NC)[:, :, 1:NC]
                for a in range(2):
                    p.tensor_tensor(x3(0, a), t3(0, a), t3(1, a), ALU.subtract).then_inc(x_ready, 1)
                    p.tensor_tensor(x3(1, a), t3(2, a), t3(3, a), ALU.add).then_inc(x_ready, 1)

        @block.scalar
        def _(act):
            s = nc.scalar
            for b in range(8):
                act.wait_ge(y_done, b + 1)
                s.activation(S.ug[:, 4 * b:4 * b + 4, :].rearrange("p g c -> p (g c)"), (y0, y1)[b % 2][:],
                             ACT.Gelu_apprx_tanh).then_inc(y_out, 1)
            for b in range(0, 8, 2):
                act.wait_ge(tr_done, b + 1)
                s.activation(yp[:, :, 4 * b * C:4 * (b + 1) * C].rearrange("p i (g c) -> p i g c", c=C),
                             t0[:].rearrange("p (g i c) -> p i g c", g=4, c=C), ACT.Copy).then_inc(tr_out_a, 1)
            for b in range(0, 8, 2):
                act.wait_ge(t2_done, b + 1)
                s.activation(yt[:, b // 2, :].rearrange("p (c i) -> p i c", i=L)[:, 0:4, :],
                             t0[:].rearrange("p (i c) -> p i c", i=4), ACT.Copy).then_inc(t2_out_a, 1)
            for b in range(8):
                act.wait_ge(g_done, b + 1)
                if b >= 2:
                    act.wait_ge(g_mul, b - 1)
                s.activation(gate[:, b % 2], (y0, y1)[b % 2][:], ACT.Sigmoid,
                             bias=S.vec[:, V_BG + b // 2:V_BG + b // 2 + 1]).then_inc(g_out, 1)


def phase_d(nc, A, S):
    S.qt = place(nc, "qt", [DQK, H, SEQ], 0)
    S.kt = place(nc, "kt", [DQK, H, SEQ], 32)
    S.v = place(nc, "v", [P, NT, DS], 64)
    wuq = place(nc, "wuq", [P, 2, H * DQK], 80)
    wukv = place(nc, "wukv", [P, H * (DN + DV)], 86)
    qs = place(nc, "qs", [P, 2, H, DQK], 135)
    kf = place(nc, "kf", [P, 2, H, DQK], 141)
    sq = place(nc, "sq", [P, H * DQK + H * DN], 147)
    tab = place(nc, "ropetab", [P, 2, 4, NT, HALF], 153)
    krr = place(nc, "krr", [P, NT, DR], 157)
    ksq = place(nc, "ksq", [P, NT, DR], 158)
    rt = place(nc, "rt", [P, 4, H, HALF], 159)
    rk = place(nc, "rk", [P, 4, NT, HALF], 161)
    HQ = 5

    with ExitStack() as ctx:
        kss = ctx.enter_context(nc.sbuf_tensor("kss", [P, NT], FP32))
        ss = ctx.enter_context(nc.sbuf_tensor("ss", [P, NT, 2 * H], FP32))
        q0, q1, k0, k1, tq0, tq1, tk0, tk1 = banks(ctx, nc, "pdd", 8)
        sem = lambda n: ctx.enter_context(nc.semaphore(n))
        w_in, proj_done, squared, reduced, std_ready = sem("d_w"), sem("d_proj"), sem("d_sq"), sem("d_red"), sem("d_std")
        q_scaled, k_scaled, q_roped, k_roped = sem("d_qsc"), sem("d_ksc"), sem("d_qro"), sem("d_kro")
        tq_done, tk_done, q_out, k_out, tab_ready = sem("d_tq"), sem("d_tk"), sem("d_qo"), sem("d_ko"), sem("d_tab")
        block = ctx.enter_context(nc.Block())
        tile = lambda i: slice(i * P, (i + 1) * P)

        @block.sync
        def _(sp):
            sp.dma_start(wuq[:], A["w_uq"][0].rearrange("(k p) n -> p k n", p=P)).then_inc(w_in, 16)
            sp.dma_start(wukv[:], A["w_ukv"][0]).then_inc(w_in, 16)

        @block.tensor
        def _(pe):
            t = nc.tensor
            pe.wait_ge(w_in, 32)
            for it in range(NT + 1):
                i = it
                if i < NT:
                    if i >= 1:
                        pe.wait_ge(squared, i)
                        pe.wait_ge(q_scaled, 2 * i)
                        pe.wait_ge(k_scaled, 2 * i)
                    for k in range(2):
                        t.matmul(q0[:, 0:HQ * DQK], S.ct[:, k, tile(i)], wuq[:, k, 0:HQ * DQK], start=k == 0, stop=k == 1)
                    for k in range(2):
                        t.matmul(q1[:, 0:(H - HQ) * DQK], S.ct[:, k, tile(i)], wuq[:, k, HQ * DQK:], start=k == 0, stop=k == 1)
                    t.matmul(k0[:], S.ct[:, 2, tile(i)], wukv[:, 0:512], start=True, stop=True)
                    t.matmul(k1[:], S.ct[:, 2, tile(i)], wukv[:, 512:], start=True, stop=True).then_inc(proj_done, 1)
                i = it - 1
                if 0 <= i:
                    pe.wait_ge(q_roped, 2 * (i + 1))
                    if i >= 1:
                        pe.wait_ge(q_out, 2 * i)
                    for h in range(H):
                        last = t.transpose((tq0, tq1)[h // 4][0:DQK, (h % 4) * P:(h % 4 + 1) * P], qs[:, i % 2, h, :], S.ident[:])
                    last.then_inc(tq_done, 1)
                    pe.wait_ge(k_roped, i + 1)
                    pe.wait_ge(k_scaled, 2 * (i + 1))
                    if i >= 1:
                        pe.wait_ge(k_out, 2 * i)
                    for h in range(H):
                        last = t.transpose((tk0, tk1)[h // 4][0:DQK, (h % 4) * P:(h % 4 + 1) * P], kf[:, i % 2, h, :], S.ident[:])
                    last.then_inc(tk_done, 1)

        @block.scalar
        def _(act):
            s = nc.scalar
            for it in range(NT + 1):
                i = it
                if i < NT:
                    act.wait_ge(proj_done, i + 1)
                    if i >= 1:
                        act.wait_ge(reduced, i)
                    s.activation(sq[:, 0:HQ * DQK], q0[:, 0:HQ * DQK], ACT.Square)
                    s.activation(sq[:, HQ * DQK:H * DQK], q1[:, 0:(H - HQ) * DQK], ACT.Square)
                    for n, bank in enumerate((k0, k1)):
                        kv = bank[:].rearrange("p (h n) -> p h n", h=4)
                        s.activation(sq[:, H * DQK + n * 4 * DN:H * DQK + (n + 1) * 4 * DN].rearrange("p (h n) -> p h n", h=4),
                                     kv[:, :, 0:DN], ACT.Square)
                        last = s.activation(S.v[:, i, n * 256:(n + 1) * 256].rearrange("p (h n) -> p h n", h=4), kv[:, :, DN:], ACT.Copy)
                    last.then_inc(squared, 1)
                    act.wait_ge(reduced, i + 1)
                    s.activation(ss[:, i, :], ss[:, i, :], ACT.Sqrt, scale=1.0 / DQK, bias=S.eps[:]).then_inc(std_ready, 1)
                i = it - 1
                if 0 <= i:
                    act.wait_ge(tq_done, i + 1)
                    for n, bank in enumerate((tq0, tq1)):
                        s.activation(S.qt[:, 4 * n:4 * n + 4, tile(i)], bank[0:DQK, :].rearrange("p (h n) -> p h n", h=4),
                                     ACT.Copy, scale=S.gcol[:, 0:1]).then_inc(q_out, 1)

        @block.vector
        def _(dve):
            v = nc.vector
            own = S.chain(dve, "dve")
            for n in range(2):
                g1 = bcast(S.gqk[:, n, DN:DN + HALF], 1, [P, NT, HALF])
                g2 = bcast(S.gqk[:, n, DN + HALF:], 1, [P, NT, HALF])
                for m, (g, fn) in enumerate(((g1, 1), (g2, 0), (g2, 1), (g1, 0))):
                    own.mark(v.tensor_tensor(tab[:, n, m], S.rope[:, fn], g, ALU.mult))
            own.mark(v.tensor_tensor(ksq[:], S.kr[:], S.kr[:], ALU.mult))
            own.wait()
            own.mark(v.tensor_reduce(kss[:], ksq[:], AX.X, ALU.add))
            x1, x2 = S.kr[:, :, 0:HALF], S.kr[:, :, HALF:]
            for m, x in enumerate((x1, x2, x2, x1)):
                own.mark(v.tensor_tensor(rk[:, m], x, tab[:, 1, m], ALU.mult))
            own.wait()
            own.mark(v.tensor_tensor(krr[:, :, 0:HALF], rk[:, 0], rk[:, 1], ALU.subtract))
            own.mark(v.tensor_tensor(krr[:, :, HALF:], rk[:, 2], rk[:, 3], ALU.add))
            own.wait()
            v.tensor_copy(rk[:, 0], tab[:, 0, 0]).then_inc(tab_ready, 1)
            for it in range(NT + 1):
                i = it
                if i < NT:
                    dve.wait_ge(squared, i + 1)
                    own.mark(v.tensor_reduce(ss[:, i, 0:H], sq[:, 0:H * DQK].rearrange("p (h n) -> p h n", h=H), AX.X, ALU.add))
                    own.step(v.tensor_reduce(ss[:, i, H:], sq[:, H * DQK:].rearrange("p (h n) -> p h n", h=H), AX.X, ALU.add))
                    v.tensor_scalar(ss[:, i, H:], ss[:, i, H:], kss[:, i:i + 1], None, ALU.add).then_inc(reduced, 1)
                    dve.wait_ge(std_ready, i + 1)
                    own.step(v.reciprocal(ss[:, i, :], ss[:, i, :]))
                    if i >= 2:
                        dve.wait_ge(tq_done, i - 1)
                        dve.wait_ge(tk_done, i - 1)
                    v.tensor_tensor(qs[:, i % 2, 0:HQ, :], q0[:, 0:HQ * DQK].rearrange("p (h n) -> p h n", n=DQK),
                                    bcast(ss[:, i, 0:HQ], 2, [P, HQ, DQK]), ALU.mult).then_inc(q_scaled, 1)
                    v.tensor_tensor(qs[:, i % 2, HQ:, :], q1[:, 0:(H - HQ) * DQK].rearrange("p (h n) -> p h n", n=DQK),
                                    bcast(ss[:, i, HQ:H], 2, [P, H - HQ, DQK]), ALU.mult).then_inc(q_scaled, 1)
                    for n, bank in enumerate((k0, k1)):
                        v.tensor_tensor(kf[:, i % 2, 4 * n:4 * n + 4, 0:DN], bank[:].rearrange("p (h n) -> p h n", h=4)[:, :, 0:DN],
                                        bcast(ss[:, i, H + 4 * n:H + 4 * n + 4], 2, [P, 4, DN]), ALU.mult).then_inc(k_scaled, 1)
                i = it - 1
                if 0 <= i:
                    dve.wait_ge(tk_done, i + 1)
                    for n, bank in enumerate((tk0, tk1)):
                        v.tensor_scalar(S.kt[:, 4 * n:4 * n + 4, tile(i)], bank[0:DQK, :].rearrange("p (h n) -> p h n", h=4),
                                        S.gcol[:, 1:2], None, ALU.mult).then_inc(k_out, 1)

        @block.gpsimd
        def _(pool):
            p = nc.gpsimd
            own = S.chain(pool, "pool")
            pool.wait_ge(tab_ready, 1)
            for i in range(NT):
                pool.wait_ge(q_scaled, 2 * (i + 1))
                if i >= 1:
                    pool.wait_ge(q_roped, 2 * i)
                x1, x2 = qs[:, i % 2, :, DN:DN + HALF], qs[:, i % 2, :, DN + HALF:]
                for m, x in enumerate((x1, x2, x2, x1)):
                    own.mark(p.tensor_tensor(rt[:, m], x, bcast(tab[:, 0, m, i, :], 1, [P, H, HALF]), ALU.mult))
                own.wait()
                p.tensor_tensor(x1, rt[:, 0], rt[:, 1], ALU.subtract).then_inc(q_roped, 1)
                p.tensor_tensor(x2, rt[:, 2], rt[:, 3], ALU.add).then_inc(q_roped, 1)
                p.tensor_tensor(kf[:, i % 2, :, DN:], bcast(krr[:, i, :], 1, [P, H, DR]),
                                bcast(ss[:, i, H:], 2, [P, H, DR]), ALU.mult).then_inc(k_roped, 1)


def phase_e(nc, A, S):
    S.yat = place(nc, "yat", [P, KS, SEQ], 119)
    S.wout = place(nc, "wout", [P, KD, D], 160)
    pex = place(nc, "pex", [P, 2, SEQ], 135)
    pts = place(nc, "pts", [P, 2, SEQ], 143)
    ya = place(nc, "ya", [P, 2, DS], 151)
    mask = place(nc, "mask", [P, P], 155)
    junk = place(nc, "junk_e", [P, DS], 156)

    SCALE = DQK ** -0.5
    items = [(i, h) for i in range(NT) for h in range(H)]

    with ExitStack() as ctx:
        top = ctx.enter_context(nc.sbuf_tensor("top", [P, NT * H], FP32))
        rsum = ctx.enter_context(nc.sbuf_tensor("rsum", [P, NT * H], FP32))
        sps = [ctx.enter_context(nc.psum_tensor(f"scores{n}", [P, SEQ], FP32)) for n in range(2)]
        ptp = ctx.enter_context(nc.psum_tensor("ptp", [P, SEQ], FP32))
        ob, tr = banks(ctx, nc, "pee", 2)
        sem = lambda n: ctx.enter_context(nc.semaphore(n))
        mask_ready, s_done, top_ready, exp_done, pt_done = sem("e_mask"), sem("e_s"), sem("e_top"), sem("e_exp"), sem("e_pt")
        pt_out_d, pt_out_a, pv_done, ya_ready = sem("e_ptd"), sem("e_pta"), sem("e_pv"), sem("e_ya")
        tr_done, tr_out = sem("e_tr"), sem("e_tro")
        w_in, scaled = sem("e_w"), sem("e_sc")
        block = ctx.enter_context(nc.Block())
        wide = lambda m: sum(1 for i, _ in items[:m] if i >= 4)

        @block.sync
        def _(sp):
            sp.dma_start(S.wout[:], A["w_out"][0].rearrange("(k p) n -> p k n", p=P)).then_inc(w_in, 16)

        @block.gpsimd
        def _(pool):
            own = S.chain(pool, "pool")
            own.step(nc.gpsimd.memset(mask[:], 0.0))
            nc.gpsimd.affine_select(out=mask[:], in_=mask[:], compare_op=ALU.is_ge, fill=-1e30, base=0,
                                    pattern=[[-1, P]], channel_multiplier=1).then_inc(mask_ready, 1)
            pool.wait_ge(w_in, 16)
            for k in range(KD):
                nc.gpsimd.tensor_scalar(S.wout[:, k], S.wout[:, k], S.vec[:, V_OS + k:V_OS + k + 1], None, ALU.mult).then_inc(scaled, 1)

        @block.tensor
        def _(pe):
            t = nc.tensor

            def scores(m):
                i, h = items[m]
                if m >= 2:
                    pe.wait_ge(exp_done, m - 1)
                n = (i + 1) * P
                for a in range(0, n, 512):
                    b = min(a + 512, n)
                    last = t.matmul(sps[m % 2][:, a:b], S.qt[:, h, i * P:(i + 1) * P], S.kt[:, h, a:b], start=True, stop=True)
                last.then_inc(s_done, 1)

            def turn(m):
                i, h = items[m]
                pe.wait_ge(exp_done, m + 1)
                if m >= 1:
                    pe.wait_ge(pt_out_d, m)
                    if wide(m):
                        pe.wait_ge(pt_out_a, wide(m))
                for b in range(i + 1):
                    last = t.transpose(ptp[:, b * P:(b + 1) * P], pex[:, m % 2, b * P:(b + 1) * P], S.ident[:])
                last.then_inc(pt_done, 1)

            def values(m):
                i, h = items[m]
                pe.wait_ge(pt_out_d, m + 1)
                if wide(m + 1):
                    pe.wait_ge(pt_out_a, wide(m + 1))
                if h == 0 and i >= 1:
                    pe.wait_ge(ya_ready, i)
                for b in range(i + 1):
                    last = t.matmul(ob[:, h * DV:(h + 1) * DV], pts[:, m % 2, b * P:(b + 1) * P], S.v[:, b, h * DV:(h + 1) * DV],
                                    start=b == 0, stop=b == i)
                last.then_inc(pv_done, 1)

            def out_turn(i):
                pe.wait_ge(ya_ready, i + 1)
                if i >= 1:
                    pe.wait_ge(tr_out, i)
                for k in range(KS):
                    last = t.transpose(tr[:, k * P:(k + 1) * P], ya[:, i % 2, k * P:(k + 1) * P], S.ident[:])
                last.then_inc(tr_done, 1)

            scores(0)
            for m in range(len(items)):
                if m + 1 < len(items):
                    scores(m + 1)
                turn(m)
                if m >= 1:
                    values(m - 1)
                if m % H == 3 and m >= H:
                    out_turn(m // H - 1)
            values(len(items) - 1)
            out_turn(NT - 1)

        @block.vector
        def _(dve):
            v = nc.vector
            own = S.chain(dve, "dve")
            dve.wait_ge(mask_ready, 1)

            def find_top(m):
                i, h = items[m]
                dve.wait_ge(s_done, m + 1)
                sc = sps[m % 2]
                own.step(v.tensor_tensor(sc[:, i * P:(i + 1) * P], sc[:, i * P:(i + 1) * P], mask[:], ALU.add))
                own.step(v.tensor_reduce(top[:, m:m + 1], sc[:, 0:(i + 1) * P], AX.X, ALU.max))
                v.tensor_scalar(top[:, m:m + 1], top[:, m:m + 1], -SCALE, None, ALU.mult).then_inc(top_ready, 1)

            def evacuate(m):
                i, h = items[m]
                dve.wait_ge(pt_done, m + 1)
                if m >= 2:
                    dve.wait_ge(pv_done, m - 1)
                w = min(i + 1, 4) * P
                v.tensor_copy(pts[:, m % 2, 0:w], ptp[:, 0:w]).then_inc(pt_out_d, 1)

            def normalise(i):
                dve.wait_ge(pv_done, H * (i + 1))
                own.step(v.reciprocal(rsum[:, i * H:(i + 1) * H], rsum[:, i * H:(i + 1) * H]))
                if i >= 2:
                    dve.wait_ge(tr_done, i - 1)
                v.tensor_tensor(ya[:, i % 2].rearrange("p (h n) -> p h n", h=H), ob[:].rearrange("p (h n) -> p h n", h=H),
                                bcast(rsum[:, i * H:(i + 1) * H], 2, [P, H, DV]), ALU.mult).then_inc(ya_ready, 1)

            find_top(0)
            for m in range(len(items)):
                if m + 1 < len(items):
                    find_top(m + 1)
                evacuate(m)
                if m % H == 1 and m >= H:
                    normalise(m // H - 1)
            normalise(NT - 1)

        @block.scalar
        def _(act):
            s = nc.scalar
            own = S.chain(act, "act")
            for m, (i, h) in enumerate(items):
                act.wait_ge(top_ready, m + 1)
                if m >= 2:
                    act.wait_ge(pt_done, m - 1)
                n = (i + 1) * P
                s.activation(pex[:, m % 2, 0:n], sps[m % 2][:, 0:n], ACT.Exp, scale=SCALE, bias=top[:, m:m + 1],
                             accum_out=rsum[:, m:m + 1]).then_inc(exp_done, 1)
                if i >= 4:
                    act.wait_ge(pt_done, m + 1)
                    act.wait_ge(pv_done, m - 1)
                    s.activation(pts[:, m % 2, 512:n], ptp[:, 512:n], ACT.Copy).then_inc(pt_out_a, 1)
                if m % H == 4 and m >= H:
                    j = m // H - 1
                    act.wait_ge(ya_ready, j + 1)
                    own.step(s.activation(junk[:], ya[:, j % 2], ACT.Square, accum_out=S.ssa[:, j:j + 1]))
                    act.wait_ge(tr_done, j + 1)
                    s.activation(S.yat[:, :, j * P:(j + 1) * P], tr[:].rearrange("p (k n) -> p k n", k=KS), ACT.Copy).then_inc(tr_out, 1)
            j = NT - 1
            act.wait_ge(ya_ready, j + 1)
            own.step(s.activation(junk[:], ya[:, j % 2], ACT.Square, accum_out=S.ssa[:, j:j + 1]))
            act.wait_ge(tr_done, j + 1)
            s.activation(S.yat[:, :, j * P:(j + 1) * P], tr[:].rearrange("p (k n) -> p k n", k=KS), ACT.Copy).then_inc(tr_out, 1)


def query_weights(A, h):
    return A["w_query"][0].rearrange("(k p) (h n) -> h p k n", p=P, n=2 * PK)[h]


def phase_f(nc, A, S):
    S.x2 = place(nc, "x2", [P, NT, D], 32)
    S.h2 = place(nc, "h2", [P, NT, D], 64)
    S.wq = place(nc, "wq", [P, PH, KD, 2 * PK], 96)
    S.sk = place(nc, "sk", [P, 2, PK], 192)
    wout = S.wout
    sq = place(nc, "sq_f", [P, KS, SEQ], 12)
    junk = place(nc, "junk_f", [P, D], 28)
    part = place(nc, "part", [P, 2, D], 135)
    S.gate_f = place(nc, "gate_f", [P, D], 195)[:]
    rowt = place(nc, "rows", [P, 3, D], 0)
    rows = [rowt[:, 0], rowt[:, 1], rowt[:, 2], S.gate_f]
    row_cols = (S.mod[:, GATE_M:GATE_M + KD], S.a_f[:], S.mod[:, SHIFT_F:SHIFT_F + KD], S.mod[:, GATE_F:GATE_F + KD])

    with ExitStack() as ctx:
        ones = ctx.enter_context(nc.sbuf_tensor("ones", [P, 1], FP32))
        rs = ctx.enter_context(nc.sbuf_tensor("rs_f", [P, 3, NT], FP32))
        ss2 = ctx.enter_context(nc.sbuf_tensor("ss_f", [P, NT], FP32))
        pa = [ctx.enter_context(nc.psum_tensor(f"outs{n}", [P, D], FP32)) for n in range(2)]
        pb = [ctx.enter_context(nc.psum_tensor(f"outa{n}", [P, D], FP32)) for n in range(2)]
        sem = lambda n: ctx.enter_context(nc.semaphore(n))
        q_in, x_in, rows_done, rows_out = sem("f_q"), sem("f_x"), sem("f_rd"), sem("f_ro")
        sq_done, ss_done, std_ready, rs_ready = sem("f_sq"), sem("f_ss"), sem("f_std"), sem("f_rs")
        mm_done, a_out, b_read, x2_ready, std2_ready = sem("f_mm"), sem("f_ao"), sem("f_br"), sem("f_x2"), sem("f_std2")
        ones_made = sem("f_ones")
        block = ctx.enter_context(nc.Block())
        tile = lambda i: slice(i * P, (i + 1) * P)

        @block.sync
        def _(sp):
            sp.dma_start(S.x2[:], A["x"][0].rearrange("(i p) d -> p i d", p=P)).then_inc(x_in, 16)
            sp.dma_start(S.sk[:], A["sub_keys"][0].rearrange("a k d -> k a d")).then_inc(q_in, 16)
            for h in range(2):
                sp.dma_start(S.wq[:, PH - 1 - h], query_weights(A, h)).then_inc(q_in, 16)
            sp.wait_ge(q_in, 48)

        @block.gpsimd
        def _(pool):
            nc.gpsimd.memset(ones[:], 1.0).then_inc(ones_made, 1)

        @block.tensor
        def _(pe):
            t = nc.tensor
            for r, bank in enumerate((pa[0], pa[1], pb[0], pb[1])):
                for k in range(KD):
                    last = t.transpose(bank[:, k * P:(k + 1) * P], row_cols[r][:, k:k + 1].to_broadcast([P, P]), S.ident[:])
                last.then_inc(rows_done, 1)
            pe.wait_ge(rows_out, 4)
            pe.wait_ge(ones_made, 1)
            pe.wait_ge(sq_done, 1)
            for i in range(NT):
                for k in range(KS):
                    last = t.matmul(pb[1][:, i:i + 1], sq[:, k, tile(i)], ones[:], start=k == 0, stop=k == KS - 1)
            last.then_inc(ss_done, 1)
            for i in range(NT):
                if i >= 2:
                    pe.wait_ge(a_out, i - 1)
                    pe.wait_ge(b_read, i - 1)
                if i == 1:
                    pe.wait_ge(std_ready, 1)
                for src, k0, out in ((S.yst, 0, pa[i % 2]), (S.yat, KS, pb[i % 2])):
                    for half in range(2):
                        for k in range(KS):
                            last = t.matmul(out[:, half * 512:(half + 1) * 512], src[:, k, tile(i)],
                                            wout[:, k0 + k, half * 512:(half + 1) * 512], start=k == 0, stop=k == KS - 1)
                last.then_inc(mm_done, 1)

        @block.scalar
        def _(act):
            s = nc.scalar
            own = S.chain(act, "act")
            s.activation(sq[:], S.yst[:], ACT.Square).then_inc(sq_done, 1)
            for r, bank in ((1, pa[1]), (3, pb[1])):
                act.wait_ge(rows_done, r + 1)
                s.activation(rows[r], bank[:], ACT.Copy).then_inc(rows_out, 1)
            s.activation(rs[:, 1, :], S.ssa[:], ACT.Sqrt, scale=1.0 / DS, bias=S.eps[:])
            act.wait_ge(ss_done, 1)
            s.activation(rs[:, 0, :], pb[1][:, 0:NT], ACT.Sqrt, scale=1.0 / DS, bias=S.eps[:]).then_inc(std_ready, 1)
            act.wait_ge(rs_ready, 1)
            for i in range(NT + 1):
                if i < NT:
                    act.wait_ge(mm_done, i + 1)
                    if i >= 2:
                        act.wait_ge(x2_ready, i - 1)
                    s.activation(part[:, i % 2], pa[i % 2][:], ACT.Copy, scale=rs[:, 0, i:i + 1]).then_inc(a_out, 1)
                j = i - 1
                if j >= 0:
                    act.wait_ge(x2_ready, j + 1)
                    own.step(s.activation(junk[:], S.x2[:, j], ACT.Square, accum_out=ss2[:, j:j + 1]))
                    s.activation(rs[:, 2, j:j + 1], ss2[:, j:j + 1], ACT.Sqrt, scale=1.0 / D, bias=S.eps[:]).then_inc(std2_ready, 1)

        @block.vector
        def _(dve):
            v = nc.vector
            own = S.chain(dve, "dve")
            for r, bank in ((0, pa[0]), (2, pb[0])):
                dve.wait_ge(rows_done, r + 1)
                v.tensor_copy(rows[r], bank[:]).then_inc(rows_out, 1)
            dve.wait_ge(std_ready, 1)
            v.reciprocal(rs[:, 0:2, :].rearrange("p a n -> p (a n)"), rs[:, 0:2, :].rearrange("p a n -> p (a n)")).then_inc(rs_ready, 1)
            dve.wait_ge(rs_ready, 1)
            dve.wait_ge(x_in, 16)
            dve.wait_ge(rows_out, 4)
            for i in range(NT + 1):
                if i < NT:
                    pt = part[:, i % 2]
                    dve.wait_ge(a_out, i + 1)
                    v.scalar_tensor_tensor(pt, pb[i % 2][:], rs[:, 1, i:i + 1], pt, ALU.mult, ALU.add).then_inc(b_read, 1)
                    dve.wait_ge(b_read, i + 1)
                    own.step(v.tensor_tensor(pt, pt, rows[0], ALU.mult))
                    v.tensor_tensor(S.x2[:, i], S.x2[:, i], pt, ALU.add).then_inc(x2_ready, 1)
                j = i - 1
                if j >= 0:
                    dve.wait_ge(std2_ready, j + 1)
                    own.step(v.reciprocal(rs[:, 2, j:j + 1], rs[:, 2, j:j + 1]))
                    own.step(v.scalar_tensor_tensor(S.h2[:, j], S.x2[:, j], rs[:, 2, j:j + 1], rows[1], ALU.mult, ALU.mult))
                    own.step(v.tensor_tensor(S.h2[:, j], S.h2[:, j], rows[2], ALU.add))


def phase_g(nc, A, S):
    ND, NU, NG = 8, 4, 4
    AHEAD = 2
    TURN = PH - AHEAD - 1
    LOWEST = -3.0e38
    PARTS = 6
    dn = place(nc, "dn", [P, ND, D], 0)
    wq = S.wq
    up = place(nc, "up_g", [P, NU, D], 160)
    h2n = place(nc, "h2n", [P, D], 176)
    h2t = place(nc, "h2t", [P, KD, P], 180)
    cand = place(nc, "cand", [P, 2, TOPK, TOPK], 184)
    hot = place(nc, "hot", [P, 2, TOPK, TOPK], 186)
    dg = place(nc, "dg", [P, NG, P], 188)
    qt = place(nc, "qt_g", [P, 2, P], 190)
    skt = place(nc, "skt", [P, 2, PK], 191)
    sk = S.sk
    s2 = place(nc, "s2", [P, 2, PK], 193)

    with ExitStack() as ctx:
        small = lambda *a: ctx.enter_context(nc.sbuf_tensor(*a))
        top_v = small("top_v", [P, 2, TOPK], FP32)
        top_i = small("top_i", [P, 2, TOPK], U32)
        top_f = small("top_f", [P, 2, TOPK], FP32)
        best = small("best", [P, TOPK], FP32)
        best_i = small("best_i", [P, TOPK], U32)
        part_i = small("part_i", [P, 2, TOPK], U32)
        part_f = small("part_f", [P, 2, TOPK], FP32)
        key = small("key", [P, 2, TOPK], FP32)
        iota_f = small("iota_f", [P, TOPK], FP32)
        idx = small("idx_g", [P, PH, TOPK], U32)
        g = small("g", [P, PH, TOPK], FP32)
        gs = small("gs", [P, PH, 2], FP32)
        a = small("a", [P, 2, TOPK], FP32)
        ga = small("ga", [P, 2, TOPK], FP32)
        w = small("w", [P, 2, TOPK], FP32)
        acc = ctx.enter_context(nc.psum_tensor("acc", [P, D], FP32))
        t0, t1, qb, sb = banks(ctx, nc, "pgg", 4)
        sem = lambda n: ctx.enter_context(nc.semaphore(n))
        dn_in = [sem(f"g_dn{n}") for n in range(ND)]
        up_in = [sem(f"g_up{n}") for n in range(NU)]
        wq_in = [sem(f"g_wq{n}") for n in range(3)]
        sk_t, sk_out, iota_made = sem("g_skt"), sem("g_sko"), sem("g_iota")
        dotted, up_used, dg_ready, ga_ready = sem("g_dot"), sem("g_upused"), sem("g_dg"), sem("g_ga")
        top_ready, exp_ready, idx_ready = sem("g_top"), sem("g_exp"), sem("g_idx")
        h2n_ready, t_done, t_out, q_done, q_out, s_done, s_read = (sem(f"g_{n}") for n in ("nx", "t", "to", "q", "qo", "s", "sr"))
        acc_read, fin_ready, stored, dve_own = sem("g_acc"), sem("g_fin"), sem("g_st"), sem("g_dve")
        block = ctx.enter_context(nc.Block())
        LAST = NT - 1

        def hold(eng, s, value):
            eng.wait_ge(s, value)
            eng.nop(nofuse=True)

        @block.sync
        def _(sp):
            for n in range(3):
                for h in (2 * n + 2, 2 * n + 3):
                    sp.dma_start(wq[:, PH - 1 - h], query_weights(A, h)).then_inc(wq_in[n], 16)
            out = A["out"][0].rearrange("(i p) d -> p i d", p=P)
            with sp.Fori(0, NT, 1) as i:
                sp.wait_ge(fin_ready, i + 1)
                sp.dma_start(out[:, bass.ds(i, 1), :], S.x2[:, bass.ds(i, 1), :]).then_inc(stored, 16)
            sp.wait_ge(stored, 16 * NT)

        @block.gpsimd
        def _(pool):
            p = nc.gpsimd
            p.iota(iota_f[:], pattern=[[1, TOPK]], base=0, channel_multiplier=0,
                   allow_small_or_imprecise_dtypes=True).then_inc(iota_made, 1)

            def down(i, h, k, free):
                if free:
                    hold(pool, dotted, P * i + (TOPK * h + k + 1 - ND))
                p.indirect_dma_start(dn[:, k % ND, :], None, A["expert_down"][0],
                                     bass.IndirectOffsetOnAxis(ap=idx[:, h % PH, k:k + 1], axis=0)).then_inc(dn_in[k % ND], 16)

            def fetch_up(i, h, k, free):
                if free:
                    hold(pool, up_used, P * i + (TOPK * h + k + 1 - NU))
                p.indirect_dma_start(up[:, k % NU, :], None, A["expert_up"][0],
                                     bass.IndirectOffsetOnAxis(ap=idx[:, h, k:k + 1], axis=0)).then_inc(up_in[k % NU], 16)

            pool.wait_ge(idx_ready, 1)
            for k in range(TOPK):
                down(0, 0, k, k >= ND)

            def slot_one(i, first):
                hold(pool, idx_ready, PH * i + 2)
                for k in range(TOPK):
                    down(i, 1, k, True)
                    fetch_up(i, 0, k, k >= NU or not first)

            def slots(i):
                for s in range(2, PH + 1):
                    hold(pool, idx_ready, PH * i + s + 1)
                    for k in range(TOPK):
                        down(i, s, k, True)
                        fetch_up(i, s - 1, k, True)

            slot_one(0, True)
            slots(0)
            with pool.Fori(1, LAST, 1) as i:
                slot_one(i, False)
                slots(i)
            slot_one(LAST, False)
            for s in range(2, PH):
                hold(pool, idx_ready, PH * LAST + s + 1)
                for k in range(TOPK):
                    down(LAST, s, k, True)
                    fetch_up(LAST, s - 1, k, True)
            for k in range(TOPK):
                fetch_up(LAST, PH - 1, k, True)

        @block.tensor
        def _(pe):
            t = nc.tensor
            for n in range(2):
                last = t.transpose(t0[:, n * PK:(n + 1) * PK], sk[:, n, :], S.ident[:])
            last.then_inc(sk_t, 1)
            pe.wait_ge(sk_out, 1)

            def turn(i):
                pe.wait_ge(h2n_ready, i + 1)
                for k in range(KD):
                    last = t.transpose((t0, t1)[k // 4][:, (k % 4) * P:(k % 4 + 1) * P], h2n[:, k * P:(k + 1) * P], S.ident[:])
                last.then_inc(t_done, 1)

            def queries(i, h):
                if h == 0:
                    pe.wait_ge(t_out, 2 * i + 2)
                if isinstance(i, int) and i == 0 and h % 2 == 0 and h > 0:
                    pe.wait_ge(wq_in[h // 2 - 1], 32)
                for n in range(2):
                    for k in range(KD):
                        last = t.matmul(qb[:, n * P:(n + 1) * P], wq[:, PH - 1 - h, k, n * PK:(n + 1) * PK],
                                        h2t[:, k, :], start=k == 0, stop=k == KD - 1)
                last.then_inc(q_done, 1)

            def scores(i, h, first=False):
                pe.wait_ge(q_out, PH * i + h + 1)
                if not first:
                    pe.wait_ge(s_read, PH * i + h)
                for n in range(2):
                    last = t.matmul(sb[:, n * PK:(n + 1) * PK], qt[:, n, :], skt[:, n, :], start=True, stop=True)
                last.then_inc(s_done, 1)

            def add_up(i, h, k):
                pe.wait_ge(up_in[k % NU], (16 * P // NU) * i + 16 * ((TOPK * h + k) // NU + 1))
                pe.wait_ge(dg_ready, P * i + (TOPK * h + k + 1))
                for half in range(2):
                    last = t.matmul(acc[:, half * 512:(half + 1) * 512], dg[:, k % NG, :], up[:, k % NU, half * 512:(half + 1) * 512],
                                    start=(h == 0 and k == 0), stop=(h == PH - 1 and k == TOPK - 1), skip_group_check=True)
                last.then_inc(up_used, 1)

            def slot(i, s, find):
                ni, nh = (i, s + AHEAD) if s + AHEAD < PH else (i + 1, s + AHEAD - PH)
                if find:
                    queries(ni, nh)
                for k in range(TOPK):
                    if k == 2 and find:
                        scores(ni, nh)
                    add_up(i, s - 1, k)

            turn(0)
            for h in range(AHEAD + 1):
                queries(0, h)
                scores(0, h, h == 0)
            for s in range(1, PH + 1):
                slot(0, s, True)
                if s == TURN:
                    turn(1)
            with pe.Fori(1, LAST, 1) as i:
                for s in range(1, PH + 1):
                    if s == 1:
                        pe.wait_ge(acc_read, i)
                    slot(i, s, True)
                    if s == TURN:
                        turn(i + 1)
            pe.wait_ge(acc_read, LAST)
            for s in range(1, PH + 1):
                slot(LAST, s, s <= TURN)

        @block.scalar
        def _(act):
            s_ = nc.scalar

            def next_tile(i):
                if not isinstance(i, int) or i > 0:
                    act.wait_ge(t_done, i)
                s_.activation(h2n[:], S.h2[:, bass.ds(i, 1), :].rearrange("p a d -> p (a d)"), ACT.Copy).then_inc(h2n_ready, 1)

            def turned(i):
                act.wait_ge(t_done, i + 1)
                for n, bank in enumerate((t0, t1)):
                    s_.activation(h2t[:, 4 * n:4 * n + 4, :].rearrange("p k n -> p (k n)"), bank[:], ACT.Copy).then_inc(t_out, 1)

            def queried(i, h):
                act.wait_ge(q_done, PH * i + h + 1)
                s_.activation(qt[:].rearrange("p a n -> p (a n)"), qb[:, 0:2 * P], ACT.Copy).then_inc(q_out, 1)

            def softened(i, h):
                act.wait_ge(top_ready, PH * i + h + 1)
                s_.activation(g[:, h, :], best[:], ACT.Exp, bias=gs[:, h, 0:1], accum_out=gs[:, h, 1:2]).then_inc(exp_ready, 1)

            def gelu(i, h):
                act.wait_ge(dotted, P * i + TOPK * (h + 1))
                s_.activation(ga[:, h % 2, :], a[:, h % 2, :], ACT.Gelu_apprx_tanh).then_inc(ga_ready, 1)

            def slot(i, s, find, dots):
                ni, nh = (i, s + AHEAD) if s + AHEAD < PH else (i + 1, s + AHEAD - PH)
                if find:
                    queried(ni, nh)
                    softened(ni, nh)
                if dots:
                    gelu(i, s)

            act.wait_ge(sk_t, 1)
            s_.activation(skt[:].rearrange("p a n -> p (a n)"), t0[:, 0:2 * PK], ACT.Copy).then_inc(sk_out, 1)
            s_.activation(h2n[:], S.h2[:, 0, :], ACT.Copy).then_inc(h2n_ready, 1)
            turned(0)
            for h in range(AHEAD):
                queried(0, h)
                softened(0, h)
            slot(0, 0, True, True)
            for s in range(1, PH + 1):
                if s == TURN:
                    next_tile(1)
                slot(0, s, True, True)
                if s == TURN:
                    turned(1)
            with act.Fori(1, LAST, 1) as i:
                for s in range(1, PH + 1):
                    if s == TURN:
                        next_tile(i + 1)
                    slot(i, s, True, True)
                    if s == TURN:
                        turned(i + 1)
            for s in range(1, PH):
                slot(LAST, s, s <= TURN, True)

        @block.vector
        def _(dve):
            v = nc.vector
            own = Chain(dve, dve_own)
            dve.wait_ge(iota_made, 1)

            def find_half(i, h, n):
                if n == 0:
                    hold(dve, s_done, PH * i + h + 1)
                sc = sb[:, n * PK:(n + 1) * PK]
                own.step(v.max(out=top_v[:, n, 0:8], in_=sc))
                own.mark(v.max_index(out=top_i[:, n, 0:8], in_max=top_v[:, n, 0:8], in_values=sc))
                own.step(v.match_replace(out=s2[:, n, :], in_to_replace=top_v[:, n, 0:8], in_values=sc, imm_value=LOWEST))
                own.step(v.max(out=top_v[:, n, 8:16], in_=s2[:, n, :]))
                own.mark(v.max_index(out=top_i[:, n, 8:16], in_max=top_v[:, n, 8:16], in_values=s2[:, n, :]))

            c, c2 = cand[:, 0].rearrange("p a b -> p (a b)"), cand[:, 1].rearrange("p a b -> p (a b)")

            def find_sums(i, h):
                own.wait()
                own.mark(v.tensor_copy(top_f[:], top_i[:]))
                v.tensor_tensor(cand[:, 0], bcast(top_v[:, 0, :], 2, [P, TOPK, TOPK]), bcast(top_v[:, 1, :], 1, [P, TOPK, TOPK]),
                                ALU.add).then_inc(s_read, 1)
                hold(dve, s_read, PH * i + h + 1)
                own.step(v.max(out=best[:, 0:8], in_=c))
                own.mark(v.max_index(out=best_i[:, 0:8], in_max=best[:, 0:8], in_values=c))
                own.mark(v.tensor_scalar(gs[:, h, 0:1], best[:, 0:1], -1.0, None, ALU.mult))

            def find_more_sums(i, h):
                own.step(v.match_replace(out=c2, in_to_replace=best[:, 0:8], in_values=c, imm_value=LOWEST))
                v.max(out=best[:, 8:16], in_=c2).then_inc(top_ready, 1)
                hold(dve, top_ready, PH * i + h + 1)
                own.step(v.max_index(out=best_i[:, 8:16], in_max=best[:, 8:16], in_values=c2))
                own.mark(v.tensor_scalar(part_i[:, 0, :], best_i[:], 4, None, ALU.logical_shift_right))
                own.step(v.tensor_scalar(part_i[:, 1, :], best_i[:], TOPK - 1, None, ALU.bitwise_and))
                own.mark(v.tensor_copy(part_f[:], part_i[:]))

            def find_keys():
                own.wait()
                for n in range(2):
                    own.mark(v.tensor_tensor(hot[:, n], bcast(part_f[:, n, :], 2, [P, TOPK, TOPK]),
                                             bcast(iota_f[:], 1, [P, TOPK, TOPK]), ALU.is_equal))

            def find_experts(i, h, reused):
                own.wait()
                for n in range(2):
                    own.mark(v.tensor_tensor(hot[:, n], hot[:, n], bcast(top_f[:, n, :], 1, [P, TOPK, TOPK]), ALU.mult))
                own.wait()
                own.step(v.tensor_reduce(key[:], hot[:], AX.X, ALU.add))
                if reused:
                    dve.wait_ge(up_used, P * i + TOPK * (h - PH + 1))
                v.scalar_tensor_tensor(idx[:, h, :], key[:, 0, :], float(PK), key[:, 1, :], ALU.mult, ALU.add).then_inc(idx_ready, 1)

            def find_weights(i, h):
                dve.wait_ge(exp_ready, PH * i + h + 1)
                own.step(v.reciprocal(gs[:, h, 1:2], gs[:, h, 1:2]))
                own.mark(v.tensor_scalar(g[:, h, :], g[:, h, :], gs[:, h, 1:2], None, ALU.mult))

            def find_part(m, i, h, reused=True):
                if m < 2:
                    find_half(i, h, m)
                elif m == 2:
                    find_sums(i, h)
                elif m == 3:
                    find_more_sums(i, h)
                elif m == 4:
                    find_keys()
                elif m == 5:
                    find_experts(i, h, reused)
                else:
                    find_weights(i, h)

            def dot(i, h, k):
                row = (i + h // PH) if isinstance(i, int) else i + h // PH
                dve.wait_ge(dn_in[k % ND], (16 * P // ND) * i + 16 * ((TOPK * h + k) // ND + 1))
                v.scalar_tensor_tensor(dn[:, k % ND, :], dn[:, k % ND, :], 1.0, S.h2[:, bass.ds(row, 1), :].rearrange("p a d -> p (a d)"),
                                       ALU.mult, ALU.mult, accum_out=a[:, h % 2, k:k + 1]).then_inc(dotted, 1)

            def diagonal(i, h, k, first=False):
                if not first:
                    dve.wait_ge(up_used, P * i + (TOPK * h + k + 1 - NG))
                v.tensor_scalar(dg[:, k % NG, :], S.ident[:], w[:, h % 2, k:k + 1], None, ALU.mult).then_inc(dg_ready, 1)

            def weigh(i, h):
                own.wait()
                dve.wait_ge(ga_ready, PH * i + h + 1)
                own.step(v.tensor_tensor(w[:, h % 2, :], ga[:, h % 2, :], g[:, h % PH, :], ALU.mult))

            def slot(i, s, finds, dots, first=False):
                ni, nh = (i, s + AHEAD) if s + AHEAD < PH else (i + 1, s + AHEAD - PH)
                for k in range(TOPK):
                    diagonal(i, s - 1, k, first and k < NG)
                    if dots:
                        dot(i, s, k)
                    if finds and 3 <= k < 3 + PARTS + 1:
                        find_part(k - 3, ni, nh, not (isinstance(ni, int) and ni == 0))
                if dots:
                    weigh(i, s)

            def finish(i):
                dve.wait_ge(up_used, P * i + P)
                tmp = S.h2[:, bass.ds(i, 1), :].rearrange("p a d -> p (a d)")
                v.tensor_tensor(tmp, acc[:], S.gate_f, ALU.mult).then_inc(acc_read, 1)
                dve.wait_ge(acc_read, i + 1)
                x = S.x2[:, bass.ds(i, 1), :].rearrange("p a d -> p (a d)")
                v.tensor_tensor(x, x, tmp, ALU.add).then_inc(fin_ready, 1)

            def restart():
                own.wait()
                dve.sem_clear(dve_own)
                own.n = 0

            for m in range(PARTS + 1):
                find_part(m, 0, 0, False)
            for k in range(TOPK):
                dot(0, 0, k)
                if k < PARTS + 1:
                    find_part(k, 0, 1, False)
            for m in range(PARTS + 1):
                find_part(m, 0, 2, False)
            weigh(0, 0)
            for s in range(1, PH + 1):
                slot(0, s, True, True, s == 1)
            finish(0)
            restart()
            with dve.Fori(1, LAST, 1) as i:
                for s in range(1, PH + 1):
                    slot(i, s, True, True)
                finish(i)
                restart()
            for s in range(1, PH + 1):
                slot(LAST, s, s <= TURN, s < PH)
            finish(LAST)


INS = ['x', 'c', 'positions', 'w_ada', 'b_ada', 'norm_mix', 'norm_ffn', 'w_in', 'lam_re', 'lam_im', 'log_dt',
       'b_re', 'b_im', 'c_re', 'c_im', 'd_skip', 'w_glu', 'b_glu', 'q_a_norm', 'w_uq', 'kv_a_norm', 'w_ukv',
       'q_norm', 'k_norm', 'out_norm_ssm', 'out_norm_attn', 'w_out', 'w_query', 'sub_keys', 'expert_down', 'expert_up']


def program(nc, A):
    S = Store(nc)
    for phase in (phase_a, phase_b, phase_c, phase_d, phase_e, phase_f, phase_g):
        phase(nc, A, S)


def kernel(**inputs):
    import concourse.bacc as bacc
    from concourse.bass_utils import run_bass_kernel_spmd

    nc = bacc.Bacc("TRN2", target_bir_lowering=False, num_devices=1)
    arrays, A = {}, {}
    for name in INS:
        a = np.ascontiguousarray(inputs[name])
        arrays[f"in_{name}_dram"] = a
        A[name] = nc.dram_tensor(f"in_{name}_dram", a.shape, mybir.dt.from_np(a.dtype), kind="ExternalInput").ap()
    A["out"] = nc.dram_tensor("out_0_dram", (1, SEQ, D), FP32, kind="ExternalOutput").ap()
    program(nc, A)
    result = run_bass_kernel_spmd(nc, [arrays], core_ids=[0])
    return result.results[0]["out_0_dram"]
```
